# Optimizing a Trainium2 kernel written in Bass

```python
import math
import jax, jax.numpy as jnp
from jax import lax
import numpy as np

D_MODEL = 1024
BATCH = 1
SEQ = 2048
DEPTH = 1
DEC_BATCH = 1
DEC_SEQ = 64
PAST_LEN = 512

CHUNK = 64
D_MIX = D_MODEL
D_SSD = D_MIX // 2
P_SSD = 64
H_SSD = D_SSD // P_SSD
G_SSD = 2
HG_SSD = H_SSD // G_SSD
N_STATE = 64
CONV_W = 4
D_CONV = D_SSD + 2 * G_SSD * N_STATE
D_ATT = D_MIX - D_SSD
HD_ATT = 64
H_ATT = D_ATT // HD_ATT
Q_BLOCK = 128
D_IN = D_SSD + D_CONV + H_SSD + 3 * D_ATT + H_ATT
N_EGROUPS = 4
EXPERTS_PER_GROUP = 4
N_EXPERTS = N_EGROUPS * EXPERTS_PER_GROUP
TOP_K = 2
D_EXPERT = D_MODEL // 2
MOE_BLOCK = 256
EPS = 1e-6
NEG_BIG = -1e30

kernel_name = 'hymba_ssd_fox_hmoe_stream_step'

def rmsnorm(x, w):
    xf = x.astype(jnp.float32)
    xf = xf * lax.rsqrt(jnp.mean(xf * xf, axis=-1, keepdims=True) + EPS)
    return (xf * w.astype(jnp.float32)).astype(x.dtype)

def causal_conv(xbc, prev, w, b):
    L = xbc.shape[1]
    xpad = jnp.concatenate([prev.astype(xbc.dtype), xbc], axis=1)
    out = b + xpad[:, 0:L] * w[0]
    for i in range(1, CONV_W):
        out = out + xpad[:, i:i + L] * w[i]
    return out, xpad[:, xpad.shape[1] - (CONV_W - 1):]

def ssd_scan(x, dA, Bm, Cm, h0):
    Bn, L = x.shape[0], x.shape[1]
    pad = (-L) % CHUNK
    if pad:
        padw = lambda a: jnp.pad(a, [(0, 0), (0, pad)] + [(0, 0)] * (a.ndim - 2))
        x, dA, Bm, Cm = padw(x), padw(dA), padw(Bm), padw(Cm)
    nc = (L + pad) // CHUNK
    x = x.reshape(Bn, nc, CHUNK, G_SSD, HG_SSD, P_SSD)
    dA = dA.reshape(Bn, nc, CHUNK, G_SSD, HG_SSD)
    Bm = Bm.reshape(Bn, nc, CHUNK, G_SSD, N_STATE)
    Cm = Cm.reshape(Bn, nc, CHUNK, G_SSD, N_STATE)
    a_cum = jnp.cumsum(dA, axis=2)
    causal = jnp.tril(jnp.ones((CHUNK, CHUNK), bool))[:, :, None, None]
    seg = a_cum[:, :, :, None] - a_cum[:, :, None, :]
    decay = jnp.exp(jnp.where(causal, seg, -jnp.inf))
    cb = jnp.einsum('bctgn,bcsgn->bctsg', Cm, Bm)
    y_diag = jnp.einsum('bctsg,bctsgh,bcsghp->bctghp', cb, decay, x)
    decay_to_end = jnp.exp(a_cum[:, :, -1:] - a_cum)
    chunk_states = jnp.einsum('bcsgn,bcsgh,bcsghp->bcghpn', Bm, decay_to_end, x)
    chunk_decay = jnp.exp(a_cum[:, :, -1])

    def step(h, inp):
        cs, cd = inp
        return h * cd[..., None, None] + cs, h

    h_final, h_in = lax.scan(step, h0, (jnp.moveaxis(chunk_states, 1, 0), jnp.moveaxis(chunk_decay, 1, 0)))
    h_in = jnp.moveaxis(h_in, 0, 1)
    y_off = jnp.einsum('bctgn,bcghpn,bctgh->bctghp', Cm, h_in, jnp.exp(a_cum))
    y = (y_diag + y_off).reshape(Bn, nc * CHUNK, G_SSD, HG_SSD, P_SSD)[:, :L]
    return y, h_final

def fox_attention(q, k, v, Fq, Fk, q_pos, k_pos):
    Bn, Lq, H, Dh = q.shape
    blk = min(Q_BLOCK, Lq)
    nb = Lq // blk
    scale = Dh ** -0.5
    kf = k.astype(jnp.float32)
    vf = v.astype(jnp.float32)
    Fk_t = jnp.swapaxes(Fk, 1, 2)
    qb = jnp.moveaxis(q.reshape(Bn, nb, blk, H, Dh), 1, 0)
    Fqb = jnp.moveaxis(Fq.reshape(Bn, nb, blk, H), 1, 0)
    pb = q_pos.reshape(nb, blk)

    def one_block(args):
        qi, Fi, pi = args
        s = jnp.einsum('bqhd,bkhd->bhqk', qi.astype(jnp.float32), kf) * scale
        s = s + (jnp.swapaxes(Fi, 1, 2)[..., :, None] - Fk_t[..., None, :])
        s = jnp.where(k_pos[None, None, None, :] <= pi[None, None, :, None], s, NEG_BIG)
        p = jax.nn.softmax(s, axis=-1)
        return jnp.einsum('bhqk,bkhd->bqhd', p, vf)

    o = lax.map(one_block, (qb, Fqb, pb))
    return jnp.moveaxis(o, 0, 1).reshape(Bn, Lq, H, Dh)

def mixer(h, k_prev, v_prev, logf_prev, conv_prev, ssm_prev, w_in, conv_w, conv_b, dt_bias, a_log,
          d_skip, ssd_norm_w, f_bias, attn_norm_w, w_out):
    Bn, L, _ = h.shape
    f32 = jnp.float32
    proj = h @ w_in
    i0 = D_SSD
    i1 = i0 + D_CONV
    i2 = i1 + H_SSD
    i3 = i2 + D_ATT
    i4 = i3 + D_ATT
    i5 = i4 + D_ATT
    z, xbc, dt_raw = proj[..., :i0], proj[..., i0:i1], proj[..., i1:i2]
    q, k, v, f_raw = proj[..., i2:i3], proj[..., i3:i4], proj[..., i4:i5], proj[..., i5:]
    xbc_c, new_conv = causal_conv(xbc, conv_prev, conv_w, conv_b)
    xbc_c = jax.nn.silu(xbc_c.astype(f32))
    xs = xbc_c[..., :D_SSD].reshape(Bn, L, G_SSD, HG_SSD, P_SSD)
    Bm = xbc_c[..., D_SSD:D_SSD + G_SSD * N_STATE].reshape(Bn, L, G_SSD, N_STATE)
    Cm = xbc_c[..., D_SSD + G_SSD * N_STATE:].reshape(Bn, L, G_SSD, N_STATE)
    dt = jax.nn.softplus(dt_raw.astype(f32) + dt_bias.astype(f32)).reshape(Bn, L, G_SSD, HG_SSD)
    A = -jnp.exp(a_log.astype(f32)).reshape(G_SSD, HG_SSD)
    h0 = ssm_prev.astype(f32).reshape(Bn, G_SSD, HG_SSD, P_SSD, N_STATE)
    y, h_fin = ssd_scan(xs * dt[..., None], dt * A, Bm, Cm, h0)
    y = y + d_skip.astype(f32).reshape(G_SSD, HG_SSD)[:, :, None] * xs
    y = y.reshape(Bn, L, D_SSD) * jax.nn.silu(z.astype(f32))
    y_ssd = rmsnorm(y, ssd_norm_w)
    new_ssm = h_fin.reshape(Bn, H_SSD, P_SSD, N_STATE)
    q = q.reshape(Bn, L, H_ATT, HD_ATT)
    k = k.reshape(Bn, L, H_ATT, HD_ATT)
    v = v.reshape(Bn, L, H_ATT, HD_ATT)
    logf = jax.nn.log_sigmoid(f_raw.astype(f32) + f_bias.astype(f32))
    p0 = k_prev.shape[1]
    k_all = jnp.concatenate([k_prev.astype(k.dtype), k], axis=1)
    v_all = jnp.concatenate([v_prev.astype(v.dtype), v], axis=1)
    F_all = jnp.cumsum(jnp.concatenate([logf_prev.astype(f32), logf], axis=1), axis=1)
    o = fox_attention(q, k_all, v_all, F_all[:, p0:], F_all, p0 + jnp.arange(L), jnp.arange(p0 + L))
    y_att = rmsnorm(o.reshape(Bn, L, D_ATT), attn_norm_w)
    out = jnp.concatenate([y_ssd, y_att], axis=-1).astype(h.dtype) @ w_out
    return out, (k, v, logf, new_conv, new_ssm)

def hier_moe(h, w_rg, b_rg, w_re, b_re, w_gate, w_up, w_down):
    T, D = h.shape
    f32 = jnp.float32
    hf = h.astype(f32)
    p_group = jax.nn.softmax(hf @ w_rg.astype(f32) + b_rg.astype(f32), axis=-1)
    p_sel, g_sel = lax.top_k(p_group, 1)
    p_sel, g_sel = p_sel[:, 0], g_sel[:, 0]
    logits_in = jnp.einsum('td,gde->tge', hf, w_re.astype(f32)) + b_re.astype(f32)
    l_sel = jnp.take_along_axis(logits_in, g_sel[:, None, None], axis=1)[:, 0]
    top_l, top_i = lax.top_k(l_sel, TOP_K)
    w_top = jax.nn.softmax(top_l, axis=-1) * p_sel[:, None]
    expert = g_sel[:, None] * EXPERTS_PER_GROUP + top_i
    A = T * TOP_K
    e_flat = expert.reshape(A)
    w_flat = w_top.reshape(A)
    tok_flat = jnp.repeat(jnp.arange(T, dtype=jnp.int32), TOP_K)
    order = jnp.argsort(e_flat)
    e_sorted = e_flat[order]
    counts = jnp.zeros((N_EXPERTS,), jnp.int32).at[e_flat].add(1)
    padded = (counts + MOE_BLOCK - 1) // MOE_BLOCK * MOE_BLOCK
    start = jnp.cumsum(counts) - counts
    pend = jnp.cumsum(padded)
    pstart = pend - padded
    dest = pstart[e_sorted] + (jnp.arange(A, dtype=jnp.int32) - start[e_sorted])
    nb = -(-(A + N_EXPERTS * (MOE_BLOCK - 1)) // MOE_BLOCK)
    P = nb * MOE_BLOCK
    tok_sorted = tok_flat[order]
    rows_x = jnp.zeros((P, D), h.dtype).at[dest].set(h[tok_sorted])
    rows_tok = jnp.full((P,), T, jnp.int32).at[dest].set(tok_sorted)
    rows_w = jnp.zeros((P,), f32).at[dest].set(w_flat[order])
    blk_start = jnp.arange(nb, dtype=jnp.int32) * MOE_BLOCK
    blk_expert = jnp.minimum(jnp.searchsorted(pend, blk_start, side='right'), N_EXPERTS - 1)

    def run_block(args):
        xb, e = args
        return (jax.nn.silu(xb @ w_gate[e]) * (xb @ w_up[e])) @ w_down[e]

    out = lax.map(run_block, (rows_x.reshape(nb, MOE_BLOCK, D), blk_expert)).reshape(P, D)
    y = jax.ops.segment_sum(out.astype(f32) * rows_w[:, None], rows_tok, num_segments=T + 1)[:T]
    return y.astype(h.dtype)

def block(x, c, k_prev, v_prev, logf_prev, conv_prev, ssm_prev, lw):
    (norm1_w, w_ada, b_ada, w_in, conv_w, conv_b, dt_bias, a_log, d_skip, ssd_norm_w, f_bias,
     attn_norm_w, w_out, norm2_w, w_rg, b_rg, w_re, b_re, w_gate, w_up, w_down) = lw
    Bn, L, D = x.shape
    mod = (jax.nn.silu(c) @ w_ada + b_ada)[:, None, :]
    sh1, sc1, g1, sh2, sc2, g2 = jnp.split(mod, 6, axis=-1)
    h = rmsnorm(x, norm1_w) * (1 + sc1) + sh1
    m, states = mixer(h, k_prev, v_prev, logf_prev, conv_prev, ssm_prev, w_in, conv_w, conv_b, dt_bias,
                      a_log, d_skip, ssd_norm_w, f_bias, attn_norm_w, w_out)
    x = x + g1 * m
    h = rmsnorm(x, norm2_w) * (1 + sc2) + sh2
    x = x + g2 * hier_moe(h.reshape(Bn * L, D), w_rg, b_rg, w_re, b_re, w_gate, w_up, w_down).reshape(Bn, L, D)
    return x, states

def setup_inputs(seed: int = 0) -> dict:
    key = jax.random.key(seed)
    ks = iter(jax.random.split(key, 48))
    f32 = jnp.float32
    nrm = lambda shape, s: jax.random.normal(next(ks), shape, f32) * s
    x_prompt = nrm((BATCH, SEQ, D_MODEL), 1.0)
    x_sample = nrm((DEC_BATCH, DEC_SEQ, D_MODEL), 1.0)
    c_prompt = nrm((BATCH, D_MODEL), 1.0)
    c_sample = nrm((DEC_BATCH, D_MODEL), 1.0)
    cache_k = nrm((DEPTH, DEC_BATCH, PAST_LEN, H_ATT, HD_ATT), 1.0)
    cache_v = nrm((DEPTH, DEC_BATCH, PAST_LEN, H_ATT, HD_ATT), 1.0)
    cache_logf = jax.nn.log_sigmoid(3.0 + nrm((DEPTH, DEC_BATCH, PAST_LEN, H_ATT), 1.0))
    state_conv = nrm((DEPTH, DEC_BATCH, CONV_W - 1, D_CONV), 1.0)
    state_ssm = nrm((DEPTH, DEC_BATCH, H_SSD, P_SSD, N_STATE), 0.1)
    norm1_w = 1.0 + nrm((DEPTH, D_MODEL), 0.02)
    w_ada = nrm((DEPTH, D_MODEL, 6 * D_MODEL), 0.5 * D_MODEL ** -0.5)
    b_ada = nrm((DEPTH, 6 * D_MODEL), 0.01)
    w_in = nrm((DEPTH, D_MODEL, D_IN), D_MODEL ** -0.5)
    conv_w = nrm((DEPTH, CONV_W, D_CONV), CONV_W ** -0.5)
    conv_b = nrm((DEPTH, D_CONV), 0.01)
    dt0 = jnp.exp(jax.random.uniform(next(ks), (DEPTH, H_SSD), f32, math.log(1e-3), math.log(1e-1)))
    dt_bias = dt0 + jnp.log(-jnp.expm1(-dt0))
    a_log = jnp.log(jax.random.uniform(next(ks), (DEPTH, H_SSD), f32, 1.0, 16.0))
    d_skip = 1.0 + nrm((DEPTH, H_SSD), 0.02)
    ssd_norm_w = 1.0 + nrm((DEPTH, D_SSD), 0.02)
    f_bias = jax.random.uniform(next(ks), (DEPTH, H_ATT), f32, 1.0, 5.0)
    attn_norm_w = 1.0 + nrm((DEPTH, D_ATT), 0.02)
    w_out = nrm((DEPTH, D_MIX, D_MODEL), D_MIX ** -0.5)
    norm2_w = 1.0 + nrm((DEPTH, D_MODEL), 0.02)
    w_rg = nrm((DEPTH, D_MODEL, N_EGROUPS), D_MODEL ** -0.5)
    b_rg = nrm((DEPTH, N_EGROUPS), 0.01)
    w_re = nrm((DEPTH, N_EGROUPS, D_MODEL, EXPERTS_PER_GROUP), D_MODEL ** -0.5)
    b_re = nrm((DEPTH, N_EGROUPS, EXPERTS_PER_GROUP), 0.01)
    w_gate = nrm((DEPTH, N_EXPERTS, D_MODEL, D_EXPERT), D_MODEL ** -0.5)
    w_up = nrm((DEPTH, N_EXPERTS, D_MODEL, D_EXPERT), D_MODEL ** -0.5)
    w_down = nrm((DEPTH, N_EXPERTS, D_EXPERT, D_MODEL), D_EXPERT ** -0.5)
    final_norm_w = 1.0 + nrm((D_MODEL,), 0.02)
    w_ada_f = nrm((D_MODEL, 2 * D_MODEL), 0.5 * D_MODEL ** -0.5)
    b_ada_f = nrm((2 * D_MODEL,), 0.01)
    return {'x_prompt': x_prompt, 'x_sample': x_sample, 'c_prompt': c_prompt, 'c_sample': c_sample,
            'cache_k': cache_k, 'cache_v': cache_v, 'cache_logf': cache_logf,
            'state_conv': state_conv, 'state_ssm': state_ssm,
            'norm1_w': norm1_w, 'w_ada': w_ada, 'b_ada': b_ada, 'w_in': w_in, 'conv_w': conv_w,
            'conv_b': conv_b, 'dt_bias': dt_bias, 'a_log': a_log, 'd_skip': d_skip,
            'ssd_norm_w': ssd_norm_w, 'f_bias': f_bias, 'attn_norm_w': attn_norm_w, 'w_out': w_out,
            'norm2_w': norm2_w, 'w_rg': w_rg, 'b_rg': b_rg, 'w_re': w_re, 'b_re': b_re,
            'w_gate': w_gate, 'w_up': w_up, 'w_down': w_down,
            'final_norm_w': final_norm_w, 'w_ada_f': w_ada_f, 'b_ada_f': b_ada_f}

def reference(x_prompt, x_sample, c_prompt, c_sample, cache_k, cache_v, cache_logf, state_conv, state_ssm,
              norm1_w, w_ada, b_ada, w_in, conv_w, conv_b, dt_bias, a_log, d_skip, ssd_norm_w, f_bias,
              attn_norm_w, w_out, norm2_w, w_rg, b_rg, w_re, b_re, w_gate, w_up, w_down,
              final_norm_w, w_ada_f, b_ada_f):
    dtype = x_prompt.dtype
    bp = x_prompt.shape[0]
    k0 = jnp.zeros((bp, 0, H_ATT, HD_ATT), dtype)
    lf0 = jnp.zeros((bp, 0, H_ATT), jnp.float32)
    conv0 = jnp.zeros((bp, CONV_W - 1, D_CONV), dtype)
    ssm0 = jnp.zeros((bp, H_SSD, P_SSD, N_STATE), jnp.float32)
    yp, ys = x_prompt, x_sample
    kp, vp, lfp, cvp, smp = [], [], [], [], []
    ks_, vs_, lfs, cvs, sms = [], [], [], [], []
    for l in range(DEPTH):
        lw = (norm1_w[l], w_ada[l], b_ada[l], w_in[l], conv_w[l], conv_b[l], dt_bias[l], a_log[l], d_skip[l],
              ssd_norm_w[l], f_bias[l], attn_norm_w[l], w_out[l], norm2_w[l], w_rg[l], b_rg[l], w_re[l],
              b_re[l], w_gate[l], w_up[l], w_down[l])
        yp, (k_n, v_n, lf_n, cv_n, sm_n) = block(yp, c_prompt, k0, k0, lf0, conv0, ssm0, lw)
        kp.append(k_n); vp.append(v_n); lfp.append(lf_n); cvp.append(cv_n); smp.append(sm_n)
        ys, (k_n, v_n, lf_n, cv_n, sm_n) = block(ys, c_sample, cache_k[l], cache_v[l], cache_logf[l],
                                                 state_conv[l], state_ssm[l], lw)
        ks_.append(k_n); vs_.append(v_n); lfs.append(lf_n); cvs.append(cv_n); sms.append(sm_n)
    mod_p = (jax.nn.silu(c_prompt) @ w_ada_f + b_ada_f)[:, None, :]
    mod_s = (jax.nn.silu(c_sample) @ w_ada_f + b_ada_f)[:, None, :]
    sh_p, sc_p = jnp.split(mod_p, 2, axis=-1)
    sh_s, sc_s = jnp.split(mod_s, 2, axis=-1)
    y_prompt = rmsnorm(yp, final_norm_w) * (1 + sc_p) + sh_p
    y_sample = rmsnorm(ys, final_norm_w) * (1 + sc_s) + sh_s
    return (y_prompt, y_sample,
            jnp.stack(kp), jnp.stack(vp), jnp.stack(lfp), jnp.stack(cvp), jnp.stack(smp),
            jnp.stack(ks_), jnp.stack(vs_), jnp.stack(lfs), jnp.stack(cvs), jnp.stack(sms))


_drawn_inputs = setup_inputs


def setup_inputs(seed=0):
    import zlib

    import numpy as np

    out = dict(_drawn_inputs(seed))
    spreads = {}
    factors = {'cache_logf': 4.269,
     'conv_b': 3.377,
     'd_skip': 8.0,
     'ssd_norm_w': 8.0,
     'attn_norm_w': 8.0,
     'norm2_w': 5.647,
     'b_rg': 8.0,
     'b_re': 42.964,
     'final_norm_w': 2.89,
     'b_ada_f': 4.154}
    for name, (base, spread) in spreads.items():
        noise = np.random.default_rng([zlib.crc32(name.encode()), seed]).standard_normal(out[name].shape)
        drawn = base * np.exp(spread * noise) if base else spread * noise
        out[name] = __import__('jax').numpy.asarray(drawn.astype(out[name].dtype))
    for name, factor in factors.items():
        out[name] = (out[name] * factor).astype(out[name].dtype)
    return out
```

```python
from contextlib import ExitStack

import concourse.bass as bass
from concourse import mybir

F32 = mybir.dt.float32
F32R = mybir.dt.float32r
I32 = mybir.dt.int32
U32 = mybir.dt.uint32
ACT = mybir.ActivationFunctionType
ALU = mybir.AluOpType
AX = mybir.AxisListType

P = 128
D = 1024
KD = D // P
SEQ = 2048
DEC = 64
PAST = 512
NT_P = SEQ // P
NT = NT_P + 1
NT_K = NT + PAST // P
TP = NT * P
TK = NT_K * P
H = 8
HD = 64
NST = 64
DS = 512
DC = 768
NC = DC // P
CW = 4
CA = DS + DC
C_DT = CA
C_Q = C_DT + H
C_F = C_Q + 3 * DS
WA = CA + 2 * H
WB = 3 * DS
NE = 16
NG = 4
FE = 512
EPS = 1e-6
NEG = -1e30
R = NE + NG
NBLK = 48
NSLOT = NBLK * P

V_BADA, V_N1, V_N2, V_NF, V_SSDW, V_ATTW, V_CW, V_CB, V_ALL = 0, 64, 72, 80, 88, 92, 96, 120, 126
M_SH1, M_SC1, M_G1, M_SH2, M_SC2, M_G2, M_SHF, M_SCF = range(0, 64, 8)


def stage_semaphores(nc, ctx, prefix):
    handles = []

    def give_back():
        nc.clear_and_free_semaphores(handles)
        nc.all_engine_barrier()

    ctx.callback(give_back)

    def sem(name):
        handles.append(nc.alloc_semaphore(prefix + name))
        return handles[-1]

    return sem


def constants(nc, c):
    with nc.Block() as block:

        @block.gpsimd
        def _(pool):
            nc.gpsimd.memset(c.ident[:], 0.0)
            nc.gpsimd.memset(c.ones[:], 1.0)
            nc.gpsimd.memset(c.zeros[:], 0.0).then_inc(c.const_filled, 1)
            pool.wait_ge(c.const_filled, 1)
            nc.gpsimd.affine_select(out=c.ident[:], in_=c.zeros[:], compare_op=ALU.not_equal, fill=1.0,
                                    base=0, pattern=[[-1, P]], channel_multiplier=1)
            nc.gpsimd.affine_select(out=c.tri[:], in_=c.ones[:], compare_op=ALU.is_ge, fill=0.0,
                                    base=0, pattern=[[1, P]], channel_multiplier=-1)
            nc.gpsimd.affine_select(out=c.tri_strict[:], in_=c.ones[:], compare_op=ALU.is_ge, fill=0.0,
                                    base=-1, pattern=[[1, P]], channel_multiplier=-1)
            nc.gpsimd.affine_select(out=c.neg_ts[:], in_=c.zeros[:], compare_op=ALU.is_ge, fill=NEG,
                                    base=0, pattern=[[1, P]], channel_multiplier=-1)
            nc.gpsimd.affine_select(out=c.neg_qk[:], in_=c.zeros[:], compare_op=ALU.is_ge, fill=NEG,
                                    base=0, pattern=[[-1, P]], channel_multiplier=1)
            nc.gpsimd.memset(c.sign[:, 0:H], 1.0)
            nc.gpsimd.memset(c.sign[:, H:2 * H], -1.0)


def modulation(nc, c, a):
    CH = 512
    with ExitStack() as ctx:
        sb = lambda n, s, d=F32: ctx.enter_context(nc.sbuf_tensor(n, s, d))
        crow = sb("crow", [16, P])
        srow = sb("srow", [16, P])
        cT = sb("cT", [P, 16])
        vrow = sb("vrow", [V_ALL, P])
        wa = sb("wa", [P, 2, KD, CH])
        mod_rows = sb("mod_rows", [P, P])
        sem = stage_semaphores(nc, ctx, "m_")
        small_loaded, params_loaded, wada_loaded = sem("small_loaded"), sem("params_loaded"), [sem("wada0"), sem("wada1")]
        c_silu, small_T, small_copied = sem("c_silu"), sem("small_T"), sem("small_copied")
        mod_done, mod_copied, mod_biased, mod_scaled = sem("mod_done"), sem("mod_copied"), sem("mod_biased"), sem("mod_scaled")
        modrow_T, modrow_copied, modrow_stored, negA = sem("modrow_T"), sem("modrow_copied"), sem("modrow_stored"), sem("negA")
        ps = [ctx.enter_context(nc.psum_tensor(f"mod_ps{i}", [P, 512], F32)) for i in range(3)]
        wsrc = a["w_ada"][0].rearrange("(k p) n -> p k n", p=P)
        wfsrc = a["w_ada_f"].rearrange("(k p) n -> p k n", p=P)
        row = lambda x: x.rearrange("(j p) -> j p", p=P)
        block = ctx.enter_context(nc.Block())

        @block.sync
        def _(sp):
            sp.dma_start(crow[0:8, :], row(a["c_prompt"][0])).then_inc(small_loaded, 16)
            sp.dma_start(crow[8:16, :], row(a["c_sample"][0])).then_inc(small_loaded, 16)
            for at, src in ((V_BADA, a["b_ada"][0]), (V_BADA + 48, a["b_ada_f"]), (V_N1, a["norm1_w"][0]),
                            (V_N2, a["norm2_w"][0]), (V_NF, a["final_norm_w"]), (V_SSDW, a["ssd_norm_w"][0]),
                            (V_ATTW, a["attn_norm_w"][0]), (V_CB, a["conv_b"][0])):
                n = src.shape[0] // P
                sp.dma_start(vrow[at:at + n, :], row(src)).then_inc(small_loaded, 16)
            sp.dma_start(vrow[V_CW:V_CB, :], a["conv_w"][0].rearrange("i (j p) -> (i j) p", p=P)).then_inc(small_loaded, 16)
            with sp.Fori(0, 6) as i:
                for s in range(2):
                    sp.wait_ge(mod_done, i * 2 + s + 1)
                    sp.dma_start(wa[:, s], wsrc[:, :, bass.ds((i * 2 + s) * CH, CH)]).then_inc(wada_loaded[s], 16)
            for n in range(4):
                sp.wait_ge(mod_done, 13 + n)
                sp.dma_start(wa[:, n % 2], wfsrc[:, :, n * CH:(n + 1) * CH]).then_inc(wada_loaded[n % 2], 16)
            sp.wait_ge(modrow_copied, 1)
            sp.dma_start(c.mod_dram, mod_rows[:]).then_inc(modrow_stored, 16)
            sp.wait_ge(modrow_stored, 16)

        @block.gpsimd
        def _(pool):
            for at, name in ((0, "dt_bias"), (H, "f_bias"), (2 * H, "a_log"), (3 * H, "d_skip")):
                pool.dma_start(c.params[:, at:at + H], a[name].broadcast_to([P, H])).then_inc(params_loaded, 16)
            pool.dma_start(c.b_router[:, 0:NG], a["b_rg"].broadcast_to([P, NG])).then_inc(params_loaded, 16)
            pool.dma_start(c.b_router[:, NG:R], a["b_re"].rearrange("a g e -> a (g e)").broadcast_to([P, NE])).then_inc(params_loaded, 16)
            pool.wait_ge(params_loaded, 96)

        @block.scalar
        def _(act):
            act.wait_ge(small_loaded, 16 * 11)
            act.activation(srow[:], crow[:], ACT.Silu).then_inc(c_silu, 1)
            act.wait_ge(params_loaded, 96)
            act.activation(c.neg_a[:], c.params[:, 2 * H:3 * H], ACT.Exp).then_inc(negA, 1)
            act.wait_ge(negA, 1)
            act.mul(c.neg_a[:], c.neg_a[:], -1.0)

        @block.tensor
        def _(pe):
            pe.sem_inc(mod_done, 2)
            pe.wait_ge(c_silu, 1)
            pe.transpose(ps[2][:, 0:16], srow[:], c.ident[0:16, 0:16])
            pe.transpose(ps[2][:, 128:128 + V_ALL], vrow[:], c.ident[0:V_ALL, 0:V_ALL]).then_inc(small_T, 1)
            pe.wait_ge(small_copied, 1)

            def chunk(n, s, loaded):
                pe.wait_ge(wada_loaded[s], loaded)
                pe.wait_ge(mod_copied, n + 1)
                for j in range(4):
                    for k in range(KD):
                        last = pe.matmul(ps[s][:, 2 * j:2 * j + 2], wa[:, s, k, j * P:(j + 1) * P], cT[:, k:16:8],
                                         start=(k == 0), stop=(k == KD - 1))
                last.then_inc(mod_done, 1)

            with pe.Fori(0, 6) as i:
                for s in range(2):
                    chunk(i * 2 + s, s, i * 16 + 16)
            for n in range(12, 16):
                chunk(n, n % 2, 16 * (n // 2 + 1))
            pe.wait_ge(mod_scaled, 6)
            pe.transpose(ps[2][:, 256:384], c.mod_t[:].rearrange("p g j -> p (g j)"), c.ident[:]).then_inc(modrow_T, 1)

        @block.vector
        def _(dve):
            dve.sem_inc(mod_copied, 2)
            dve.wait_ge(small_T, 1)
            dve.tensor_copy(c.vcol[:], ps[2][:, 128:128 + V_ALL])
            dve.tensor_copy(cT[:], ps[2][:, 0:16]).then_inc(small_copied, 1)

            def chunk(n, s):
                dve.wait_ge(mod_done, n + 3)
                dve.tensor_copy(c.mod_t[:, :, bass.ds(n * 4, 4)].rearrange("p g j -> p j g"),
                                ps[s][:, 0:8].rearrange("p (j g) -> p j g", g=2)).then_inc(mod_copied, 1)

            with dve.Fori(0, 6) as i:
                for s in range(2):
                    chunk(i * 2 + s, s)
            for n in range(12, 16):
                chunk(n, n % 2)
            dve.wait_ge(mod_copied, 18)
            for g in range(2):
                dve.tensor_tensor(c.mod_t[:, g, :], c.mod_t[:, g, :], c.vcol[:, 0:64], ALU.add).then_inc(mod_biased, 1)
            dve.wait_ge(mod_biased, 2)
            for g in range(2):
                for m, v in ((M_SC1, V_N1), (M_SC2, V_N2), (M_SCF, V_NF)):
                    dve.scalar_tensor_tensor(out=c.mod_t[:, g, m:m + 8], in0=c.mod_t[:, g, m:m + 8], scalar=1.0,
                                             in1=c.vcol[:, v:v + 8], op0=ALU.add, op1=ALU.mult).then_inc(mod_scaled, 1)
            dve.wait_ge(modrow_T, 1)
            dve.tensor_copy(mod_rows[:], ps[2][:, 256:384]).then_inc(modrow_copied, 1)


def load_split_weights(ctx, nc, sem, tag, chunks, w_hi, w_lo, width):
    stage = ctx.enter_context(nc.sbuf_tensor(f"{tag}_stage", [P, 2, width], F32))
    loaded = [sem(f"stage_loaded{s}") for s in range(2)]
    rounded = sem("weights_rounded")
    split = sem("weights_split")
    n_dma = len(chunks[0])

    def load(sp):
        for k in range(KD):
            if k >= 2:
                sp.wait_ge(split, k - 1)
            for lo, hi, src in chunks[k]:
                sp.dma_start(stage[:, k % 2, lo:hi], src).then_inc(loaded[k % 2], 16)

    def round_hi(act):
        for k in range(KD):
            act.wait_ge(loaded[k % 2], 16 * n_dma * (k // 2 + 1))
            act.activation(w_hi[:, k, :], stage[:, k % 2, :], ACT.Copy).then_inc(rounded, 1)

    def take_lo(dve):
        for k in range(KD):
            dve.wait_ge(rounded, k + 1)
            dve.tensor_tensor(w_lo[:, k, :], stage[:, k % 2, :], w_hi[:, k, :].bitcast(F32), ALU.subtract).then_inc(split, 1)

    return load, round_hi, take_lo, split


def product3(pe, out, a_hi, a_lo, b_hi, b_lo, start, stop):
    pe.matmul(out, a_hi, b_hi, start=start, stop=False)
    pe.matmul(out, a_hi, b_lo, start=False, stop=False)
    return pe.matmul(out, a_lo, b_hi, start=False, stop=stop)


def ssd_branch(nc, c, a):
    GW = WA // 3
    with ExitStack() as ctx:
        sb = lambda n, s, d=F32: ctx.enter_context(nc.sbuf_tensor(n, s, d))
        sem = stage_semaphores(nc, ctx, "a_")
        w_hi, w_lo = sb("wa_hi", [P, KD, WA], F32R), sb("wa_lo", [P, KD, WA], F32R)
        x, xn, junk = sb("x", [P, D]), sb("xn", [P, D]), sb("junk", [P, D])
        st = sb("st", [P, 8])
        h32 = sb("h32", [P, KD, P])
        h_hi, h_lo = sb("ah_hi", [P, KD, P], F32R), sb("ah_lo", [P, KD, P], F32R)
        zx = sb("zx", [P, WA])
        xraw = sb("xraw", [P, NC, CW - 1 + P])
        conv, xbc = sb("conv", [P, NC, P]), sb("xbc", [P, NC, P])
        zs = sb("zs", [P, DS])
        t16 = sb("t16", [P, 10, 2 * H])
        lf = sb("lf", [P, H])
        dt, dA = sb("dt", [P, H]), sb("dA", [P, H])
        e_in, e_out = sb("e_in", [P, 3 * H]), sb("e_out", [P, 3 * H])
        xs, xdt, xw = sb("xs", [P, DS]), sb("xdt", [P, DS]), sb("xw", [P, DS])
        b_tok = sb("b_tok", [P, P])
        seg, mm = sb("seg", [P, H, P]), sb("mm", [P, H, P])
        y, yskip = sb("y", [P, DS]), sb("yskip", [P, DS])
        state, cdl = sb("state", [P, DS]), sb("cdl", [P, 4])
        ssm_rows, ssm0 = sb("ssm_rows", [P, 2, P]), sb("ssm0", [P, 2, P])
        pb = lambda n, w: ctx.enter_context(nc.psum_tensor(n, [P, w], F32))
        p_h, p_zx, p_xs, p_s, p_y = pb("p_h", 1024), pb("p_zx", 1536), pb("p_xs", 512), pb("p_s", 512), pb("p_y", 512)
        p_hv = p_h[:].rearrange("p (k t) -> p k t", t=P)
        p_acum, p_cb, p_lft = p_s[:, 0:2 * H], (p_s[:, 16:16 + P], p_y[:, P:2 * P]), p_s[0:H, 272:400]

        (x_loaded, ssq_ready, ms_ready, ln_ready, rs_ready, xn_ready, xT_done, h32_act, h32_dve, hhi_ready, hlo_ready,
         h_stored, proj_done, zx_ready, xbc_T, xraw_ready, zs_ready, conv_step, conv_ready, carried, xbc_ready, dt_step,
         dt_exp, dt_ln, dt_ready, lf_stored) = map(sem, (
            "x_loaded", "ssq_ready", "ms_ready", "ln_ready", "rs_ready", "xn_ready", "xT_done", "h32_act", "h32_dve",
            "hhi_ready", "hlo_ready", "h_stored", "proj_done", "zx_ready", "xbc_T", "xraw_ready", "zs_ready", "conv_step",
            "conv_ready", "carried", "xbc_ready", "dt_step", "dt_exp", "dt_ln", "dt_ready", "lf_stored"))
        (xs_T, btok_T, s_done, at_done, xs_ready, btok_ready, ein_step, ein_ready, e_ready, seg_ready, decay_ready, m_ready,
         xdt_ready, xw_ready, yd_done, yo_done, sm_done, y_step, y_ready, y_stored, st_step, st_ready, lft_ready) = map(sem, (
            "xs_T", "btok_T", "s_done", "at_done", "xs_ready", "btok_ready", "ein_step", "ein_ready", "e_ready", "seg_ready",
            "decay_ready", "m_ready", "xdt_ready", "xw_ready", "yd_done", "yo_done", "sm_done", "y_step", "y_ready",
            "y_stored", "st_step", "st_ready", "lft_ready"))
        (x_zeroed, carry_zeroed, conv_out, conv_in, ssm_in, ssm_T, ssm_copied, ssm_stored, ssm0_T, ssm0_copied) = map(sem, (
            "x_zeroed", "carry_zeroed", "conv_out", "conv_in", "ssm_in", "ssm_T", "ssm_copied", "ssm_stored", "ssm0_T",
            "ssm0_copied"))

        chunks = [[(0, CA + H, a["w_in"][0][k * P:(k + 1) * P, 0:CA + H]),
                   (CA + H, WA, a["w_in"][0][k * P:(k + 1) * P, C_F:C_F + H])] for k in range(KD)]
        block = ctx.enter_context(nc.Block())
        load, round_hi, take_lo, split = load_split_weights(ctx, nc, sem, "wa", chunks, w_hi, w_lo, WA)
        LAST = NT - 1

        @block.sync
        def _(sp):
            sp.dma_start(x[:], a["x_prompt"][0, 0:P, :]).then_inc(x_loaded, 16)
            load(sp)
            sp.sem_inc(y_stored, 16)
            for j in range(2):
                for g in range(2):
                    sp.dma_start(ssm0[:, j, g * NST:(g + 1) * NST],
                                 a["state_ssm"][0, 0][4 * g + 2 * j:4 * g + 2 * j + 2].rearrange("b p n -> (b p) n")).then_inc(ssm_in, 16)

            def step(i, nxt=True, front=True, back=True):
                if nxt:
                    sp.wait_ge(xn_ready, i + 1)
                    if isinstance(i, int) and i == LAST - 1:
                        sp.wait_ge(x_zeroed, 1)
                        sp.dma_start(x[0:DEC, :], a["x_sample"][0]).then_inc(x_loaded, 16)
                    else:
                        sp.dma_start(x[:], a["x_prompt"][0, bass.ds(i * P + P, P), :]).then_inc(x_loaded, 16)
                if front:
                    sp.wait_ge(hlo_ready, i * 2 + 2)
                    flat = lambda t: t[:].rearrange("p k t -> p (k t)").bitcast(F32)
                    sp.dma_start(c.h_hi[bass.ds(i, 1)].rearrange("o p d -> (o p) d"), flat(h_hi)).then_inc(h_stored, 16)
                    sp.dma_start(c.h_lo[bass.ds(i, 1)].rearrange("o p d -> (o p) d"), flat(h_lo)).then_inc(h_stored, 16)
                if back:
                    sp.wait_ge(y_ready, i + 1)
                    sp.dma_start(c.mix[bass.ds(i * 1 - 1, 1), :, 0:DS].rearrange("o p d -> (o p) d"), y[:]).then_inc(y_stored, 16)
                if front:
                    sp.wait_ge(dt_ready, i + 1)
                    if isinstance(i, int) and i == LAST:
                        sp.dma_start(a["logf_sample"][0, 0], lf[0:DEC, :]).then_inc(lf_stored, 16)
                    else:
                        sp.dma_start(a["logf_prompt"][0, 0, bass.ds(i * P, P), :], lf[:]).then_inc(lf_stored, 16)

            def ssm_store(n, dst):
                sp.wait_ge(ssm_copied, n)
                for j in range(2):
                    for g in range(2):
                        sp.dma_start(dst[0, 0][4 * g + 2 * j:4 * g + 2 * j + 2].rearrange("b p n -> (b p) n"),
                                     ssm_rows[:, j, g * NST:(g + 1) * NST]).then_inc(ssm_stored, 16)

            step(0, back=False)
            with sp.Fori(1, LAST - 1) as i:
                step(i)
            step(LAST - 1)
            sp.wait_ge(zx_ready, 3 * LAST)
            sp.dma_start(a["conv_prompt"][0, 0], zx[P - CW + 1:P, DS:CA]).then_inc(conv_out, 16)
            sp.wait_ge(carried, LAST)
            with nc.allow_non_contiguous_dma(reason="three rows"):
                for q in range(NC):
                    sp.dma_start(xraw[:, q, 0:CW - 1], a["state_conv"][0, 0].rearrange("i (q p) -> q p i", p=P)[q]).then_inc(conv_in, 16)
            step(LAST, nxt=False)
            sp.dma_start(a["conv_sample"][0, 0], zx[DEC - CW + 1:DEC, DS:CA]).then_inc(conv_out, 16)
            ssm_store(1, a["ssm_prompt"])
            step(NT, nxt=False, front=False)
            ssm_store(2, a["ssm_sample"])
            sp.wait_ge(conv_out, 32)
            sp.wait_ge(ssm_stored, 128)
            sp.wait_ge(y_stored, 16 * (NT + 1))
            sp.wait_ge(h_stored, 32 * NT)
            sp.wait_ge(lf_stored, 16 * NT)

        @block.tensor
        def _(pe):
            def turn_x(i, back):
                pe.wait_ge(xn_ready, i + 2)
                if back:
                    pe.wait_ge(seg_ready, i)
                for k in range(KD):
                    last = pe.transpose(p_h[:, k * P:(k + 1) * P], xn[:, k * P:(k + 1) * P], c.ident[:])
                last.then_inc(xT_done, 1)

            def project(i, g, back):
                if back:
                    pe.wait_ge(zx_ready, i * 3 - 2 + g)
                for k in range(KD):
                    if g == 0 and k % 4 == 0:
                        pe.wait_ge(hlo_ready, i * 2 + 1 + k // 4)
                    cols = slice(g * GW, (g + 1) * GW)
                    last = product3(pe, p_zx[:, g * 512:g * 512 + GW], h_hi[:, k, :], h_lo[:, k, :], w_hi[:, k, cols], w_lo[:, k, cols],
                                    k == 0, k == KD - 1)
                last.then_inc(proj_done, 1)

            def step(i, nxt=True, front=True, back=True):
                if front:
                    project(i, 0, back)
                    project(i, 1, back)
                if back:
                    pe.wait_ge(xbc_ready, i)
                    for q in range(4):
                        last = pe.transpose(p_xs[:, q * P:(q + 1) * P], xbc[:, q, :], c.ident[:])
                    last.then_inc(xs_T, 1)
                    pe.transpose(p_y[:, 0:P], xbc[:, 4, :], c.ident[:])
                    pe.matmul(p_cb[1], xbc[NST:, 4, :], xbc[NST:, 5, :], start=True, stop=True).then_inc(btok_T, 1)
                    pe.wait_ge(dt_ready, i)
                    pe.wait_ge(st_ready, i)
                    pe.matmul(p_s[:, 0:H], c.tri[:], dA[:], start=True, stop=True)
                    pe.matmul(p_s[:, H:2 * H], c.ones[:], dA[:], start=True, stop=True)
                    pe.matmul(p_cb[0], xbc[0:NST, 4, :], xbc[0:NST, 5, :], start=True, stop=True)
                    pe.transpose(p_lft, lf[:], c.ident[:]).then_inc(s_done, 1)
                    for hh in range(H):
                        last = pe.matmul(p_h[:, hh * P:(hh + 1) * P], dA[:, hh:hh + 1].to_broadcast([P, P]), c.tri[:],
                                         start=True, stop=True)
                    last.then_inc(at_done, 1)
                if front:
                    project(i, 2, back)
                if nxt:
                    turn_x(i, back)
                if back:
                    pe.wait_ge(m_ready, i)
                    pe.wait_ge(xdt_ready, i)
                    pe.wait_ge(xs_ready, i)
                    for hh in range(H):
                        cols = slice(hh * HD, (hh + 1) * HD)
                        last = pe.matmul(p_xs[:, cols], mm[:, hh, :], xdt[:, cols], start=True, stop=True)
                    last.then_inc(yd_done, 1)
                    pe.wait_ge(btok_ready, i)
                    pe.matmul(p_y[:], xbc[:, 5, :], state[:], start=True, stop=True).then_inc(yo_done, 1)
                    pe.wait_ge(xw_ready, i)
                    pe.wait_ge(lft_ready, i)
                    pe.matmul(p_s[:], b_tok[:], xw[:], start=True, stop=True).then_inc(sm_done, 1)
                if front:
                    pe.wait_ge(zx_ready, i * 3 + 3)
                    if nxt:
                        pe.wait_ge(h32_act, i + 2)
                        pe.wait_ge(h32_dve, i + 2)
                    elif back:
                        pe.wait_ge(seg_ready, i)
                    for q in range(NC):
                        last = pe.transpose(p_h[:, q * P:(q + 1) * P], zx[:, DS + q * P:DS + (q + 1) * P], c.ident[:])
                    last.then_inc(xbc_T, 1)

            def ssm_out(tiles):
                pe.wait_ge(st_ready, tiles + 1)
                pe.wait_ge(y_ready, tiles + 1)
                for g in range(2):
                    for j in range(2):
                        at = (2 * g + j) * P
                        last = pe.transpose(p_y[:, at:at + P], state[:, at:at + P], c.ident[:])
                last.then_inc(ssm_T, 1)

            turn_x(-1, back=False)
            pe.wait_ge(split, KD)
            step(0, back=False)
            with pe.Fori(1, LAST - 1) as i:
                step(i)
            step(LAST - 1)
            step(LAST, nxt=False)
            ssm_out(LAST)
            pe.wait_ge(ssm_in, 64)
            for j in range(2):
                last = pe.transpose(p_xs[:, j * P:(j + 1) * P], ssm0[:, j, :], c.ident[:])
            last.then_inc(ssm0_T, 1)
            pe.wait_ge(ssm0_copied, 1)
            pe.wait_ge(ssm_copied, 1)
            step(NT, nxt=False, front=False)
            ssm_out(NT)

        @block.scalar
        def _(act):
            def scale(i):
                act.wait_ge(x_loaded, i * 16 + 32)
                act.activation(junk[:], x[:], ACT.Square, accum_out=st[:, 0:1]).then_inc(ssq_ready, 1)
                act.wait_ge(ms_ready, i + 2)
                act.activation(st[:, 2:3], st[:, 1:2], ACT.Ln).then_inc(ln_ready, 1)
                act.wait_ge(ln_ready, i + 2)
                act.activation(st[:, 3:4], st[:, 2:3], ACT.Exp, scale=-0.5).then_inc(rs_ready, 1)

            def modulate(i, group, first=False):
                act.wait_ge(xT_done, i + 2)
                for k in range(KD // 2):
                    last = act.activation(h32[:, k, :], p_hv[:, k, :], ACT.Identity, bias=c.mod_t[:, group, M_SH1 + k:M_SH1 + k + 1],
                                          scale=c.mod_t[:, group, M_SC1 + k:M_SC1 + k + 1])
                last.then_inc(h32_act, 1)
                if not first:
                    act.wait_ge(proj_done, i * 3 + 3)
                    act.wait_ge(h_stored, i * 32 + 32)
                act.wait_ge(h32_act, i + 2)
                act.activation(h_hi[:, 0:4, :], h32[:, 0:4, :], ACT.Copy).then_inc(hhi_ready, 1)
                act.wait_ge(h32_dve, i + 2)
                act.activation(h_hi[:, 4:8, :], h32[:, 4:8, :], ACT.Copy).then_inc(hhi_ready, 1)

            def step(i, nxt=True, front=True, back=True, group=0):
                if nxt:
                    scale(i)
                if back:
                    act.wait_ge(conv_ready, i)
                    if not (isinstance(i, int) and i == 1):
                        act.wait_ge(yo_done, i - 1)
                    act.activation(xbc[:], conv[:], ACT.Silu).then_inc(xbc_ready, 1)
                    act.wait_ge(xs_T, i)
                    act.activation(xs[:], p_xs[:], ACT.Copy).then_inc(xs_ready, 1)
                    act.wait_ge(btok_T, i)
                    act.activation(b_tok[:], p_y[:, 0:P], ACT.Copy).then_inc(btok_ready, 1)
                    act.wait_ge(ein_ready, i)
                    act.activation(e_out[:], e_in[:], ACT.Exp).then_inc(e_ready, 1)
                    act.wait_ge(seg_ready, i)
                    act.activation(seg[:], seg[:], ACT.Exp).then_inc(decay_ready, 1)
                if front:
                    for g in range(3):
                        act.wait_ge(proj_done, i * 3 + 1 + g)
                        if back and g == 0:
                            act.wait_ge(xbc_T, i)
                            act.wait_ge(dt_step, i * 9)
                            if isinstance(i, int) and i == LAST:
                                act.wait_ge(conv_out, 16)
                        act.activation(zx[:, g * GW:(g + 1) * GW], p_zx[:, g * 512:g * 512 + GW], ACT.Copy).then_inc(zx_ready, 1)
                if nxt:
                    modulate(i, group)
                if front:
                    act.wait_ge(zx_ready, i * 3 + 3)
                    act.wait_ge(dt_step, i * 9 + 3)
                    act.activation(t16[:, 3, :], t16[:, 2, :], ACT.Exp, scale=-1.0).then_inc(dt_exp, 1)
                    act.wait_ge(dt_step, i * 9 + 4)
                    act.activation(t16[:, 5, :], t16[:, 4, :], ACT.Ln).then_inc(dt_ln, 1)
                    act.wait_ge(xbc_T, i + 1)
                    if back:
                        act.wait_ge(carried, i)
                    act.activation(xraw[:, :, CW - 1:], p_hv[:, 0:NC, :], ACT.Copy).then_inc(xraw_ready, 1)
                    if back:
                        act.wait_ge(y_ready, i + 1)
                    act.activation(zs[:], zx[:, 0:DS], ACT.Silu).then_inc(zs_ready, 1)

            def ssm_out(n):
                act.wait_ge(ssm_T, n)
                if n > 1:
                    act.wait_ge(ssm_stored, 64)
                for g in range(2):
                    cols = slice(g * NST, (g + 1) * NST)
                    last = act.activation(ssm_rows[:, :, cols], p_y[:, g * 256:(g + 1) * 256].rearrange("p (j n) -> p j n", n=P)[:, :, cols], ACT.Copy)
                last.then_inc(ssm_copied, 1)

            scale(-1)
            modulate(-1, 0, first=True)
            round_hi(act)
            step(0, back=False)
            with act.Fori(1, LAST - 1) as i:
                step(i)
            step(LAST - 1, group=1)
            step(LAST, nxt=False)
            ssm_out(1)
            step(NT, nxt=False, front=False)
            ssm_out(2)

        @block.vector
        def _(dve):
            def normalize(i, first=False):
                dve.wait_ge(ssq_ready, i + 2)
                dve.tensor_scalar(st[:, 1:2], st[:, 0:1], 1.0 / D, EPS, ALU.mult, ALU.add).then_inc(ms_ready, 1)
                dve.wait_ge(rs_ready, i + 2)
                if not first:
                    dve.wait_ge(xT_done, i + 1)
                dve.tensor_scalar(xn[:], x[:], st[:, 3:4], None, ALU.mult).then_inc(xn_ready, 1)

            def modulate(i, group, first=False):
                dve.wait_ge(xT_done, i + 2)
                if not first:
                    dve.wait_ge(hhi_ready, i * 2 + 2)
                for k in range(KD // 2, KD):
                    last = dve.tensor_scalar(h32[:, k, :], p_hv[:, k, :], c.mod_t[:, group, M_SC1 + k:M_SC1 + k + 1],
                                             c.mod_t[:, group, M_SH1 + k:M_SH1 + k + 1], ALU.mult, ALU.add)
                last.then_inc(h32_dve, 1)
                for half in range(2):
                    ks = slice(4 * half, 4 * half + 4)
                    dve.wait_ge(hhi_ready, i * 2 + 3 + half)
                    dve.tensor_tensor(h_lo[:, ks, :], h32[:, ks, :], h_hi[:, ks, :].bitcast(F32), ALU.subtract).then_inc(hlo_ready, 1)

            def step(i, nxt=True, front=True, back=True, group=0):
                if nxt:
                    normalize(i)
                if back:
                    dve.wait_ge(xraw_ready, i)
                    if isinstance(i, int) and i == NT:
                        dve.wait_ge(conv_in, 16 * NC)
                    if not (isinstance(i, int) and i == 1):
                        dve.wait_ge(xbc_ready, i - 1)
                    for t in range(CW):
                        for q in range(NC):
                            w = c.vcol[:, V_CW + NC * t + q:V_CW + NC * t + q + 1]
                            src = xraw[:, q, t:t + P]
                            if t == 0:
                                ins = dve.tensor_scalar(conv[:, q, :], src, w, c.vcol[:, V_CB + q:V_CB + q + 1], ALU.mult, ALU.add)
                            else:
                                ins = dve.scalar_tensor_tensor(out=conv[:, q, :], in0=src, scalar=w, in1=conv[:, q, :], op0=ALU.mult, op1=ALU.add)
                        ins.then_inc(conv_step if t < CW - 1 else conv_ready, 1)
                        if t < CW - 1:
                            dve.wait_ge(conv_step, i * 3 + t - 1)
                    dve.wait_ge(conv_ready, i)
                    dve.tensor_copy(xraw[:, :, 0:CW - 1], xraw[:, :, P:P + CW - 1]).then_inc(carried, 1)
                    dve.wait_ge(s_done, i)
                    dve.tensor_copy(e_in[:, 0:2 * H], p_acum).then_inc(ein_step, 1)
                    dve.tensor_copy(c.logf_t[:, bass.ds(i * P - P, P)], p_lft).then_inc(lft_ready, 1)
                    dve.wait_ge(ein_step, i)
                    dve.tensor_tensor(e_in[:, 2 * H:], e_in[:, H:2 * H], e_in[:, 0:H], ALU.subtract).then_inc(ein_ready, 1)
                    dve.wait_ge(at_done, i)
                    for hh in range(H):
                        last = dve.scalar_tensor_tensor(out=seg[:, hh, :], in0=p_h[:, hh * P:(hh + 1) * P], scalar=e_in[:, hh:hh + 1],
                                                        in1=c.neg_ts[:], op0=ALU.subtract, op1=ALU.add)
                    last.then_inc(seg_ready, 1)
                    heads = lambda t: t.rearrange("p (h d) -> p h d", d=HD)
                    wide = lambda t: t.unsqueeze(2).to_broadcast([P, H, HD])
                    dve.wait_ge(xs_ready, i)
                    dve.tensor_tensor(heads(xdt[:]), heads(xs[:]), wide(dt[:]), ALU.mult).then_inc(xdt_ready, 1)
                    dve.tensor_tensor(heads(yskip[:]), heads(xs[:]), wide(c.params[:, 3 * H:4 * H]), ALU.mult).then_inc(y_step, 1)
                    dve.wait_ge(xdt_ready, i)
                    dve.wait_ge(e_ready, i)
                    dve.tensor_tensor(heads(xw[:]), heads(xdt[:]), wide(e_out[:, 2 * H:]), ALU.mult).then_inc(xw_ready, 1)
                    dve.wait_ge(decay_ready, i)
                    for g in range(2):
                        last = dve.tensor_tensor(mm[:, 4 * g:4 * g + 4, :], seg[:, 4 * g:4 * g + 4, :],
                                                 p_cb[g].unsqueeze(1).to_broadcast([P, 4, P]), ALU.mult)
                    last.then_inc(m_ready, 1)
                if nxt:
                    modulate(i, group)
                if back:
                    for part, (src, done) in enumerate(((p_y, yo_done), (p_xs, yd_done))):
                        dve.wait_ge(done, i)
                        if part == 0:
                            dve.wait_ge(y_stored, i * 16)
                            dve.tensor_tensor(heads(y[:]), heads(src[:]), wide(e_out[:, 0:H]), ALU.mult).then_inc(y_step, 1)
                        else:
                            dve.tensor_tensor(y[:], y[:], src[:], ALU.add).then_inc(y_step, 1)
                        dve.wait_ge(y_step, i * 4 - 2 + part)
                    dve.tensor_tensor(y[:], y[:], yskip[:], ALU.add).then_inc(y_step, 1)
                    dve.wait_ge(y_step, i * 4)
                    dve.wait_ge(zs_ready, i)
                    dve.tensor_tensor(y[:], y[:], zs[:], ALU.mult).then_inc(y_ready, 1)
                    for g in range(2):
                        rows = slice(g * NST, (g + 1) * NST)
                        last = dve.tensor_copy(cdl[rows, :], e_out[rows, H + 4 * g:H + 4 * g + 4])
                    last.then_inc(st_step, 1)
                    dve.wait_ge(st_step, i * 2 - 1)
                    for g in range(2):
                        rows = slice(g * NST, (g + 1) * NST)
                        sv = state[rows, g * 256:(g + 1) * 256].rearrange("p (h d) -> p h d", d=HD)
                        last = dve.tensor_tensor(sv, sv, cdl[rows, :].unsqueeze(2).to_broadcast([NST, 4, HD]), ALU.mult)
                    last.then_inc(st_step, 1)
                    dve.wait_ge(st_step, i * 2)
                    dve.wait_ge(sm_done, i)
                    for g in range(2):
                        rows = slice(g * NST, (g + 1) * NST)
                        sv = state[rows, g * 256:(g + 1) * 256]
                        last = dve.tensor_tensor(sv, sv, p_s[rows, g * 256:(g + 1) * 256], ALU.add)
                    last.then_inc(st_ready, 1)
                if front:
                    dve.wait_ge(zx_ready, i * 3 + 3)
                    n = 0

                    def small(build):
                        nonlocal n
                        n += 1
                        build().then_inc(dt_step, 1)
                        dve.wait_ge(dt_step, i * 9 + n)
                    t = lambda s: t16[:, s, :]
                    small(lambda: dve.tensor_tensor(t(0), zx[:, CA:WA], c.params[:, 0:2 * H], ALU.add))
                    small(lambda: dve.tensor_tensor(t(1), t(0), c.sign[:], ALU.mult))
                    small(lambda: dve.scalar_tensor_tensor(out=t(2), in0=t(1), scalar=-1.0, in1=t(1), op0=ALU.mult, op1=ALU.max))
                    dve.wait_ge(dt_exp, i + 1)
                    small(lambda: dve.tensor_scalar(t(4), t(3), 1.0, None, ALU.add))
                    small(lambda: dve.scalar_tensor_tensor(out=t(6), in0=t(4), scalar=-1.0, in1=t(3), op0=ALU.add, op1=ALU.subtract))
                    small(lambda: dve.reciprocal(t(7), t(4)))
                    small(lambda: dve.tensor_tensor(t(8), t(6), t(7), ALU.mult))
                    dve.wait_ge(dt_ln, i + 1)
                    small(lambda: dve.tensor_tensor(t(9), t(5), t(8), ALU.subtract))
                    small(lambda: dve.scalar_tensor_tensor(out=t(0), in0=t(1), scalar=0.0, in1=t(9), op0=ALU.max, op1=ALU.add))
                    if back:
                        dve.wait_ge(lf_stored, i * 16)
                    dve.tensor_scalar(lf[:], t(0)[:, H:2 * H], -1.0, None, ALU.mult)
                    rows = slice(0, P)
                    if isinstance(i, int) and i == LAST:
                        dve.memset(dt[DEC:P, :], 0.0)
                        dve.memset(dA[DEC:P, :], 0.0)
                        rows = slice(0, DEC)
                    dve.tensor_copy(dt[rows, :], t(0)[rows, 0:H])
                    dve.tensor_tensor(dA[rows, :], t(0)[rows, 0:H], c.neg_a[rows, :], ALU.mult).then_inc(dt_ready, 1)

            dve.memset(xraw[:, :, 0:CW - 1], 0.0).then_inc(conv_step, 1)
            dve.memset(state[:], 0.0).then_inc(st_ready, 1)
            dve.sem_inc(y_ready, 1)
            dve.wait_ge(conv_step, 1)
            normalize(-1, first=True)
            modulate(-1, 0, first=True)
            take_lo(dve)
            step(0, back=False)
            with dve.Fori(1, LAST - 1) as i:
                step(i)
            dve.wait_ge(xn_ready, LAST)
            dve.memset(x[DEC:P, :], 0.0).then_inc(x_zeroed, 1)
            dve.wait_ge(x_zeroed, 1)
            step(LAST - 1, group=1)
            step(LAST, nxt=False)
            dve.wait_ge(ssm0_T, 1)
            dve.wait_ge(ssm_T, 1)
            for g in range(2):
                rows = slice(g * NST, (g + 1) * NST)
                last = dve.tensor_copy(state[rows, g * 256:(g + 1) * 256], p_xs[rows, 0:256])
            last.then_inc(ssm0_copied, 1)
            dve.wait_ge(ssm0_copied, 1)
            step(NT, nxt=False, front=False)


def forget_sums(nc, c, a):
    with ExitStack() as ctx:
        sb = lambda n, s, d=F32: ctx.enter_context(nc.sbuf_tensor("f_" + n, s, d))
        sem = stage_semaphores(nc, ctx, "f_")
        ones, F = sb("ones", [H, TK]), sb("sum", [H, TK])
        hi, lo = sb("hi", [H, TK], F32R), sb("lo", [H, TK], F32R)
        nhi, nlo = sb("nhi", [H, TK]), sb("nlo", [H, TK])
        cl, clt = sb("cl", [P, PAST // P, H]), sb("clt", [H, PAST])
        ps = ctx.enter_context(nc.psum_tensor("f_ps", [P, PAST], F32))
        cl_loaded, cl_T, ones_set, cl_out, scanned, hi_ready, lo_ready, stored = map(sem, (
            "cl_loaded", "cl_T", "ones_set", "cl_out", "scanned", "hi_ready", "lo_ready", "stored"))
        block = ctx.enter_context(nc.Block())

        @block.sync
        def _(sp):
            for t in range(PAST // P):
                sp.dma_start(cl[:, t, :], a["cache_logf"][0, 0, t * P:(t + 1) * P, :]).then_inc(cl_loaded, 16)
            sp.wait_ge(ones_set, 1)
            for r in range(2):
                sp.dma_start(c.f_k[:, r, :], ones[:]).then_inc(stored, 16)
                sp.dma_start(c.f_q[:, 2 + r, :], ones[:, 0:TP]).then_inc(stored, 16)
            sp.wait_ge(lo_ready, 3)
            sp.dma_start(c.f_q[:, 0, :], hi[:, 0:TP].bitcast(F32)).then_inc(stored, 16)
            sp.dma_start(c.f_q[:, 1, :], lo[:, 0:TP].bitcast(F32)).then_inc(stored, 16)
            sp.dma_start(c.f_k[:, 2, :], nhi[:]).then_inc(stored, 16)
            sp.dma_start(c.f_k[:, 3, :], nlo[:]).then_inc(stored, 16)
            sp.wait_ge(stored, 16 * 8)

        @block.tensor
        def _(pe):
            pe.wait_ge(cl_loaded, 64)
            for t in range(PAST // P):
                last = pe.transpose(ps[0:H, t * P:(t + 1) * P], cl[:, t, :], c.ident[:])
            last.then_inc(cl_T, 1)

        @block.vector
        def _(dve):
            dve.memset(ones[:], 1.0).then_inc(ones_set, 1)
            dve.wait_ge(cl_T, 1)
            dve.tensor_copy(clt[:], ps[0:H, :]).then_inc(cl_out, 1)
            dve.wait_ge(ones_set, 1)
            dve.tensor_tensor_scan(F[:, 0:SEQ], ones[:, 0:SEQ], c.logf_t[:, 0:SEQ], 0.0, ALU.mult, ALU.add).then_inc(scanned, 1)
            dve.wait_ge(cl_out, 1)
            dve.tensor_tensor_scan(F[:, TP:TK], ones[:, TP:TK], clt[:], 0.0, ALU.mult, ALU.add).then_inc(scanned, 1)
            dve.wait_ge(scanned, 2)
            dve.tensor_tensor_scan(F[:, SEQ:TP], ones[:, SEQ:TP], c.logf_t[:, SEQ:TP], F[:, TK - 1:TK], ALU.mult, ALU.add).then_inc(scanned, 1)
            dve.wait_ge(scanned, 3)
            dve.tensor_copy(hi[:], F[:]).then_inc(hi_ready, 1)
            dve.wait_ge(hi_ready, 1)
            dve.tensor_tensor(lo[:], F[:], hi[:].bitcast(F32), ALU.subtract).then_inc(lo_ready, 1)
            dve.tensor_scalar(nhi[:], hi[:].bitcast(F32), -1.0, None, ALU.mult).then_inc(lo_ready, 1)
            dve.wait_ge(lo_ready, 1)
            dve.tensor_scalar(nlo[:], lo[:].bitcast(F32), -1.0, None, ALU.mult).then_inc(lo_ready, 1)


def qkv_projection(nc, c, a):
    N2 = 2 * P
    with ExitStack() as ctx:
        sb = lambda n, s, d=F32: ctx.enter_context(nc.sbuf_tensor("b_" + n, s, d))
        sem = stage_semaphores(nc, ctx, "b_")
        w_hi, w_lo = sb("w_hi", [P, KD, WB], F32R), sb("w_lo", [P, KD, WB], F32R)
        h_hi, h_lo = sb("h_hi", [P, 2, 2, KD, P], F32R), sb("h_lo", [P, 2, 2, KD, P], F32R)
        qk, qk_hi, qk_lo = sb("qk", [P, 8, N2]), sb("qk_hi", [P, 8, N2], F32R), sb("qk_lo", [P, 8, N2], F32R)
        v, v_hl = sb("v", [P, 2, DS]), sb("v_hl", [P, 2, H, 2 * HD], F32R)
        k_rows = sb("k_rows", [P, 2, DS])
        banks = [ctx.enter_context(nc.psum_tensor(f"b_ps{i}", [P, 512], F32)) for i in range(8)]
        h_loaded = [sem("h_loaded0"), sem("h_loaded1")]
        (col_done, col_out, v_done, v_out, kT_done, k_out, hi_ready, lo_ready, vhi_ready, vlo_ready, qk_stored, v_stored,
         rows_stored, cache_loaded) = map(sem, (
            "col_done", "col_out", "v_done", "v_out", "kT_done", "k_out", "hi_ready", "lo_ready", "vhi_ready", "vlo_ready",
            "qk_stored", "v_stored", "rows_stored", "cache_loaded"))
        chunks = [[(0, WB, a["w_in"][0][k * P:(k + 1) * P, C_Q:C_Q + WB])] for k in range(KD)]
        block = ctx.enter_context(nc.Block())
        load, round_hi, take_lo, split = load_split_weights(ctx, nc, sem, "wb", chunks, w_hi, w_lo, WB)
        NCH = SEQ // N2
        src_k = lambda t, n=2: a["cache_k"][0, 0, t * P:(t + n) * P].rearrange("(t p) h d -> p t (h d)", p=P)
        src_v = lambda t, n=2: a["cache_v"][0, 0, t * P:(t + n) * P].rearrange("(t p) h d -> p t (h d)", p=P)

        @block.sync
        def _(sp):
            def load_h(n, s, first=False, tiles=2):
                if not first:
                    sp.wait_ge(v_done, n * 2 - 2)
                for dst, src in ((h_hi, c.h_hi), (h_lo, c.h_lo)):
                    sp.dma_start(dst[:, s, 0:tiles].bitcast(F32).rearrange("p t k m -> p t (k m)"),
                                 src[bass.ds(n * 2, tiles)].rearrange("t p d -> p t d")).then_inc(h_loaded[s], 16)

            def store(n, tiles=2, cache=None):
                tok = bass.ds(n * N2, tiles * P) if cache is None else slice(TP + cache * P, TP + cache * P + N2)
                w = tiles * P
                qrows = lambda t: t.rearrange("(j p) t -> p j t", p=P)
                sp.wait_ge(lo_ready, n * 1 + 1)
                for t, dq, dk in ((qk_hi, c.q_hi, c.k_hi), (qk_lo, c.q_lo, c.k_lo)):
                    if cache is None:
                        sp.dma_start(qrows(dq)[:, :, tok], t[:, 0:4, 0:w].bitcast(F32)).then_inc(qk_stored, 16)
                    sp.dma_start(qrows(dk)[:, :, tok], t[:, 4:8, 0:w].bitcast(F32)).then_inc(qk_stored, 16 if cache is None else 32)
                sp.wait_ge(vlo_ready, n * 1 + 1)
                for t in range(2):
                    if t < tiles:
                        tile = bass.ds(n * 2 + t, 1) if cache is None else slice(NT + cache + t, NT + cache + t + 1)
                        sp.dma_start(c.v_hl[:, tile].rearrange("h o p e -> p (h o) e"), v_hl[:, t].bitcast(F32)).then_inc(v_stored, 16 * (2 if tiles == 1 else 1))
                if cache is None:
                    if tiles == 2:
                        kd = a["k_prompt"][0, 0, tok].rearrange("(t p) h d -> p t (h d)", p=P)
                        vd = a["v_prompt"][0, 0, tok].rearrange("(t p) h d -> p t (h d)", p=P)
                        ks, vs = k_rows[:], v[:]
                    else:
                        kd, vd = (a[x][0, 0].rearrange("p h d -> p (h d)") for x in ("k_sample", "v_sample"))
                        ks, vs = k_rows[0:DEC, 0], v[0:DEC, 0]
                    sp.dma_start(vd, vs).then_inc(rows_stored, 16)
                    sp.wait_ge(k_out, n * 1 + 1)
                    sp.dma_start(kd, ks).then_inc(rows_stored, 16)

            load_h(0, 0, first=True)
            load_h(1, 1, first=True)
            load(sp)
            with sp.Fori(0, NCH // 2 - 1) as m:
                for s in range(2):
                    store(m * 2 + s)
                    load_h(m * 2 + s + 2, s)
            store(NCH - 2)
            load_h(NCH, 0, tiles=1)
            store(NCH - 1)
            store(NCH, tiles=1)
            for m in range(2):
                sp.wait_ge(rows_stored, 32 * (NCH + 1 + m))
                if m:
                    sp.wait_ge(kT_done, NCH + 1 + m)
                sp.wait_ge(vlo_ready, NCH + 1 + m)
                sp.dma_start(k_rows[:], src_k(2 * m)).then_inc(cache_loaded, 16)
                sp.dma_start(v[:], src_v(2 * m)).then_inc(cache_loaded, 16)
                sp.sem_inc(rows_stored, 32)
                store(NCH + 1 + m, cache=2 * m)
            sp.wait_ge(qk_stored, 64 * (NCH + 3))
            sp.wait_ge(v_stored, 32 * (NCH + 3))
            sp.wait_ge(rows_stored, 32 * (NCH + 3))

        @block.tensor
        def _(pe):
            pe.wait_ge(split, KD)

            def chunk(n, s, loaded, first=False):
                pe.wait_ge(h_loaded[s], loaded)
                for j in range(8):
                    if not first or j >= 4:
                        pe.wait_ge(col_out, n * 8 + j - 3)
                    cols = slice(j * P, (j + 1) * P)
                    for k in range(KD):
                        last = product3(pe, banks[j % 4][:, 0:N2].rearrange("p (t m) -> p t m", m=P), w_hi[:, k, cols], w_lo[:, k, cols],
                                        h_hi[:, s, :, k, :], h_lo[:, s, :, k, :], k == 0, k == KD - 1)
                    last.then_inc(col_done, 1)
                for t in range(2):
                    if not first:
                        pe.wait_ge(v_out, n * 2 + t - 1)
                    for k in range(KD):
                        last = product3(pe, banks[4 + t][:], h_hi[:, s, t, k, :], h_lo[:, s, t, k, :], w_hi[:, k, 8 * P:], w_lo[:, k, 8 * P:],
                                        k == 0, k == KD - 1)
                    last.then_inc(v_done, 1)
                pe.wait_ge(col_out, n * 8 + 8)
                if not first:
                    pe.wait_ge(k_out, n)
                for t in range(2):
                    for j in range(4):
                        last = pe.transpose(banks[6 + t][:, j * P:(j + 1) * P], qk[:, 4 + j, t * P:(t + 1) * P], c.ident[:])
                last.then_inc(kT_done, 1)

            chunk(0, 0, 32, first=True)
            chunk(1, 1, 32)
            with pe.Fori(1, NCH // 2) as m:
                for s in range(2):
                    chunk(m * 2 + s, s, m * 32 + 32)
            chunk(NCH, 0, 32 * (NCH // 2 + 1))
            for m in range(2):
                n = NCH + 1 + m
                pe.wait_ge(cache_loaded, 32 * (m + 1))
                pe.wait_ge(k_out, n)
                for t in range(2):
                    for j in range(4):
                        last = pe.transpose(banks[6 + t][:, j * P:(j + 1) * P], k_rows[:, t, j * P:(j + 1) * P], c.ident[:])
                last.then_inc(kT_done, 1)

        @block.scalar
        def _(act):
            round_hi(act)

            def round_qkv(n, first=False, cache=False):
                if cache:
                    act.wait_ge(k_out, n + 1)
                else:
                    act.wait_ge(col_out, n * 8 + 8)
                if not first:
                    act.wait_ge(qk_stored, n * 64)
                act.activation(qk_hi[:], qk[:], ACT.Copy).then_inc(hi_ready, 1)
                if cache:
                    act.wait_ge(cache_loaded, 32 * (n - NCH))
                else:
                    act.wait_ge(v_out, n * 2 + 2)
                if not first:
                    act.wait_ge(v_stored, n * 32)
                act.activation(v_hl[:, :, :, 0:HD].rearrange("p t h d -> p (t h) d"), v[:].rearrange("p t (h d) -> p (t h) d", d=HD), ACT.Copy).then_inc(vhi_ready, 1)

            def chunk(n, first=False):
                for j in range(8):
                    act.wait_ge(col_done, n * 8 + j + 1)
                    if j == 0 and not first:
                        act.wait_ge(lo_ready, n)
                        act.wait_ge(kT_done, n)
                    act.activation(qk[:, j, :], banks[j % 4][:, 0:N2], ACT.Copy, scale=HD ** -0.5 if j < 4 else 1.0).then_inc(col_out, 1)
                for t in range(2):
                    act.wait_ge(v_done, n * 2 + t + 1)
                    if t == 0 and not first:
                        act.wait_ge(vlo_ready, n)
                        act.wait_ge(rows_stored, n * 32)
                    act.activation(v[:, t, :], banks[4 + t][:], ACT.Copy).then_inc(v_out, 1)
                round_qkv(n, first)
                act.wait_ge(kT_done, n * 1 + 1)
                for t in range(2):
                    last = act.activation(k_rows[:, t, :], banks[6 + t][:], ACT.Copy)
                last.then_inc(k_out, 1)

            chunk(0, first=True)
            with act.Fori(1, NCH + 1) as n:
                chunk(n)
            for m in range(2):
                n = NCH + 1 + m
                act.wait_ge(kT_done, n + 1)
                act.wait_ge(lo_ready, n)
                for t in range(2):
                    last = act.activation(qk[:, 4:8, t * P:(t + 1) * P], banks[6 + t][:].rearrange("p (j m) -> p j m", m=P), ACT.Copy)
                last.then_inc(k_out, 1)
                round_qkv(n, cache=True)

        @block.vector
        def _(dve):
            take_lo(dve)

            def chunk(n):
                dve.wait_ge(hi_ready, n * 1 + 1)
                dve.tensor_tensor(qk_lo[:], qk[:], qk_hi[:].bitcast(F32), ALU.subtract).then_inc(lo_ready, 1)
                dve.wait_ge(vhi_ready, n * 1 + 1)
                dve.tensor_tensor(v_hl[:, :, :, HD:].rearrange("p t h d -> p (t h) d"), v[:].rearrange("p t (h d) -> p (t h) d", d=HD),
                                  v_hl[:, :, :, 0:HD].rearrange("p t h d -> p (t h) d").bitcast(F32), ALU.subtract).then_inc(vlo_ready, 1)

            with dve.Fori(0, NCH + 3) as n:
                chunk(n)


def attention(nc, c, a):
    scale_rows = HD + 4
    chunks = [[(q, 0, q + 1, q) for q in range(4 * n, 4 * n + 4)] for n in range(NT_P // 4)]
    chunks.append([(NT_P, SEQ, 1 + PAST // P, 0)])
    units, halves, items, rounds = [], [], [], []
    for s in range(2):
        for ch in chunks:
            ci = len(rounds)
            us = []
            for (tile, k0, n, diag) in ch:
                hs = []
                for h0 in range(0, n, 8):
                    hs.append(len(halves))
                    halves.append((h0, min(8, n - h0)))
                us.append(len(units))
                units.append(dict(s=s, tile=tile, k0=k0, n=n, diag=diag, halves=hs, chunk=ci, j=len(us) - 1))
            nk = max(n for _, _, n, _ in ch)
            its = []
            for kb in range(nk):
                j0 = next(j for j, (_, _, n, _) in enumerate(ch) if kb < n)
                its.append(len(items))
                items.append(dict(kb=kb, j0=j0, s=s, chunk=ci, k0=ch[0][1], first=kb == 0, last=kb == nk - 1))
            rounds.append(dict(s=s, units=us, items=its, n=len(ch), tile0=ch[0][0]))
    NU, NH, NI, NCH = len(units), len(halves), len(items), len(rounds)
    assert NH % 2 == 0 and NI % 2 == 0 and NCH % 2 == 0

    def schedule():
        for ci in range(NCH + 1):
            us = rounds[ci]["units"] if ci < NCH else [None]
            its = rounds[ci - 1]["items"] if ci else []
            for n, u in enumerate(us):
                if u is not None:
                    yield "scores", u
                for i in its[n * len(its) // len(us):(n + 1) * len(its) // len(us)]:
                    yield "item", i
                    if items[i]["last"]:
                        yield "finish", ci - 1

    order = list(schedule())
    with ExitStack() as ctx:
        sb = lambda n, s, d=F32: ctx.enter_context(nc.sbuf_tensor("c_" + n, s, d))
        sem = stage_semaphores(nc, ctx, "c_")
        q1, q2 = sb("q1", [P, 2, TP], F32R), sb("q2", [scale_rows, 2, TP], F32R)
        k1, k2 = sb("k1", [P, 2, TK], F32R), sb("k2", [scale_rows, 2, TK], F32R)
        vv = sb("vv", [P, 2, NT_K, 2 * HD], F32R)
        pr = sb("pr", [P, 2, 4, SEQ])
        pt_hi, pt_lo = sb("pt_hi", [P, 2, 512], F32R), sb("pt_lo", [P, 2, 512], F32R)
        mx, nm, sums = sb("mx", [P, NU, 2]), sb("nm", [P, NU]), sb("sums", [P, NU, 2])
        rs, rinv = sb("rs", [P, NU]), sb("rinv", [P, NU])
        ot = sb("ot", [P, 512])
        osum, orow = sb("osum", [P, 4, HD]), sb("orow", [P, 2, NT, HD])
        p_s = [ctx.enter_context(nc.psum_tensor(f"c_ps{i}", [P, 1024], F32)) for i in range(2)]
        p_t = [ctx.enter_context(nc.psum_tensor(f"c_pt{i}", [P, 512], F32)) for i in range(2)]
        p_o = ctx.enter_context(nc.psum_tensor("c_po", [P, 512], F32))
        p_r = ctx.enter_context(nc.psum_tensor("c_po_turned", [P, 512], F32))
        loaded = [sem("loaded0"), sem("loaded1")]
        stored = [sem("stored0"), sem("stored1")]
        (s_done, masked, mx_part, mx_done, exp_done, tr_done, hi_done, lo_done, pv_done, ot_out, or_T, sum_ready, rinv_ready, osum_ready,
         o_ready, sums_zeroed) = map(sem, (
            "s_done", "masked", "mx_part", "mx_done", "exp_done", "tr_done", "hi_done", "lo_done", "pv_done", "ot_out", "or_T",
            "sum_ready", "rinv_ready", "osum_ready", "o_ready", "sums_zeroed"))
        per = {id(x): n for x, n in ((s_done, NH), (masked, NU), (mx_part, NH), (mx_done, NU), (exp_done, NH), (tr_done, NI), (hi_done, NI),
                                     (lo_done, NI), (pv_done, NI), (ot_out, NCH), (or_T, NCH), (sum_ready, NCH), (rinv_ready, NCH),
                                     (osum_ready, NCH), (o_ready, NCH))}

        def wait(eng, s, m, n):
            eng.wait_ge(s, m * per[id(s)] + (per[id(s)] + n + 1))

        def start(eng, *sems):
            for s in sems:
                eng.sem_inc(s, per[id(s)])

        block = ctx.enter_context(nc.Block())
        N_LOADS = 10
        last_item = {s: max(i for i, it in enumerate(items) if it["s"] == s) for s in range(2)}
        last_chunk = {s: max(i for i, r in enumerate(rounds) if r["s"] == s) for s in range(2)}

        @block.sync
        def _(sp):
            def load(m, s):
                rows = bass.ds(m * (2 * HD) + s * HD, HD)
                head = bass.ds(m * 2 + s, 1)
                for dst, src in ((q1[0:HD, s], c.q_hi[rows]), (q1[HD:P, s], c.q_lo[rows]), (q2[0:HD, s], c.q_hi[rows]),
                                 (q2[HD:, s], c.f_q[head].rearrange("o r t -> (o r) t")),
                                 (k1[0:HD, s], c.k_hi[rows]), (k1[HD:P, s], c.k_hi[rows]), (k2[0:HD, s], c.k_lo[rows]),
                                 (k2[HD:, s], c.f_k[head].rearrange("o r t -> (o r) t")),
                                 (vv[:, s, 0:10], c.v_hl[head, 0:10].rearrange("o t p e -> p (o t) e")),
                                 (vv[:, s, 10:], c.v_hl[head, 10:].rearrange("o t p e -> p (o t) e"))):
                    sp.dma_start(dst.bitcast(F32), src).then_inc(loaded[s], 16)

            def store(m, s):
                wait(sp, o_ready, m, last_chunk[s])
                col = bass.ds(m * (2 * HD) + (DS + s * HD), HD)
                sp.dma_start(c.mix[:, :, col].rearrange("t p d -> p t d"), orow[:, s]).then_inc(stored[s], 16)

            load(0, 0)
            load(0, 1)
            for s in range(2):
                sp.sem_inc(stored[s], 16)
            with sp.Fori(0, H // 2 - 1) as m:
                for s in range(2):
                    wait(sp, pv_done, m, last_item[s])
                    load(m + 1, s)
                    store(m, s)
            for s in range(2):
                store(H // 2 - 1, s)
            for s in range(2):
                sp.wait_ge(stored[s], 16 * (H // 2 + 1))

        @block.tensor
        def _(pe):
            start(pe, s_done, tr_done, pv_done, or_T)

            def turn(m, i):
                it = items[i]
                r = rounds[it["chunk"]]
                if it["first"]:
                    wait(pe, exp_done, m, units[r["units"][-1]]["halves"][-1])
                wait(pe, lo_done, m, i - 2)
                for j in range(it["j0"], r["n"]):
                    last = pe.transpose(p_t[i % 2][:, j * P:(j + 1) * P], pr[:, it["chunk"] % 2, j, it["kb"] * P:(it["kb"] + 1) * P], c.ident[:])
                last.then_inc(tr_done, 1)

            def times_v(m, i):
                it = items[i]
                r = rounds[it["chunk"]]
                if it["first"]:
                    wait(pe, ot_out, m, it["chunk"] - 1)
                wait(pe, lo_done, m, i)
                cols = slice(it["j0"] * P, r["n"] * P)
                kt = it["k0"] // P + it["kb"]
                parts = [(p_o[:, cols], vv[:, it["s"], kt, :], pt_hi[:, i % 2, cols]),
                         (p_o[0:HD, cols], vv[:, it["s"], kt, 0:HD], pt_lo[:, i % 2, cols])]
                for x, (out, v_part, p_part) in enumerate(reversed(parts) if it["last"] else parts):
                    last = pe.matmul(out, v_part, p_part, start=it["first"] and x == 0, stop=it["last"] and x == 1)
                last.then_inc(pv_done, 1)

            def round_(m):
                turned = -1
                for what, n in order:
                    if what == "scores":
                        u = units[n]
                        s = u["s"]
                        if u["chunk"] % (NCH // 2) == 0 and u["j"] == 0:
                            pe.wait_ge(loaded[s], m * (16 * N_LOADS) + 16 * N_LOADS)
                        for hf in u["halves"]:
                            h0, nk = halves[hf]
                            wait(pe, exp_done, m, hf - 2)
                            for b in range(0, nk, 4):
                                w = min(4, nk - b)
                                w = 2 if w == 1 and u["k0"] == 0 else w
                                out = p_s[hf % 2][:, b * P:(b + w) * P]
                                qc = slice(u["tile"] * P, (u["tile"] + 1) * P)
                                kc = slice(u["k0"] + (h0 + b) * P, u["k0"] + (h0 + b + w) * P)
                                pe.matmul(out, q2[:, s, qc], k2[:, s, kc], start=True, stop=False)
                                last = pe.matmul(out, q1[:, s, qc], k1[:, s, kc], start=False, stop=True)
                            last.then_inc(s_done, 1)
                    elif what == "item":
                        it = items[n]
                        if turned < n:
                            turn(m, n)
                            turned = n
                        if not it["last"]:
                            turn(m, n + 1)
                            turned = n + 1
                        times_v(m, n)
                    else:
                        wait(pe, ot_out, m, n)
                        wait(pe, o_ready, m, n - 1)
                        for j in range(rounds[n]["n"]):
                            last = pe.transpose(p_r[:, j * P:(j + 1) * P], ot[:, j * P:(j + 1) * P], c.ident[:])
                        last.then_inc(or_T, 1)

            with pe.Fori(0, H // 2) as m:
                round_(m)

        @block.scalar
        def _(act):
            start(act, exp_done, hi_done, ot_out)
            act.wait_ge(sums_zeroed, 1)
            with act.Fori(0, H // 2) as m:
                for what, n in order:
                    if what == "scores":
                        u = units[n]
                        if u["j"] == 0:
                            i = rounds[u["chunk"] - 2]["items"][-1]
                            wait(act, tr_done, m, i - (NI if u["chunk"] < 2 else 0))
                        wait(act, mx_done, m, n)
                        for x, hf in enumerate(u["halves"]):
                            h0, nk = halves[hf]
                            act.activation(pr[:, u["chunk"] % 2, u["j"], h0 * P:(h0 + nk) * P], p_s[hf % 2][:, 0:nk * P], ACT.Exp,
                                           bias=nm[:, n:n + 1], accum_out=sums[:, n, x:x + 1]).then_inc(exp_done, 1)
                    elif what == "item":
                        it = items[n]
                        cols = slice(it["j0"] * P, rounds[it["chunk"]]["n"] * P)
                        wait(act, tr_done, m, n)
                        wait(act, pv_done, m, n - 2)
                        act.activation(pt_hi[:, n % 2, cols], p_t[n % 2][:, cols], ACT.Copy).then_inc(hi_done, 1)
                    else:
                        wait(act, pv_done, m, rounds[n]["items"][-1])
                        wait(act, or_T, m, n - 1)
                        w = rounds[n]["n"] * P
                        act.activation(ot[:, 0:w], p_o[:, 0:w], ACT.Copy).then_inc(ot_out, 1)

        @block.vector
        def _(dve):
            start(dve, masked, mx_part, mx_done, lo_done, sum_ready, rinv_ready, osum_ready, o_ready)
            dve.memset(sums[:], 0.0).then_inc(sums_zeroed, 1)
            dve.wait_ge(sums_zeroed, 1)
            with dve.Fori(0, H // 2) as m:
                for what, n in order:
                    if what == "scores":
                        u = units[n]
                        wait(dve, exp_done, m, u["halves"][0] - 2)
                        for x, hf in enumerate(u["halves"]):
                            h0, nk = halves[hf]
                            wait(dve, s_done, m, hf)
                            if h0 <= u["diag"] < h0 + nk:
                                blk = p_s[hf % 2][:, (u["diag"] - h0) * P:(u["diag"] - h0 + 1) * P]
                                dve.tensor_tensor(blk, blk, c.neg_qk[:], ALU.add).then_inc(masked, 1)
                                wait(dve, masked, m, n)
                            one = len(u["halves"]) == 1
                            dve.tensor_reduce(nm[:, n:n + 1] if one else mx[:, n, x:x + 1], p_s[hf % 2][:, 0:nk * P], AX.X, ALU.max,
                                              negate=one).then_inc(mx_done if one else mx_part, 1)
                            if one:
                                dve.sem_inc(mx_part, 1)
                        if not one:
                            wait(dve, mx_part, m, u["halves"][-1])
                            dve.tensor_reduce(nm[:, n:n + 1], mx[:, n, :], AX.X, ALU.max, negate=True).then_inc(mx_done, 1)
                    elif what == "item":
                        it = items[n]
                        cols = slice(it["j0"] * P, rounds[it["chunk"]]["n"] * P)
                        wait(dve, hi_done, m, n)
                        dve.tensor_tensor(pt_lo[:, n % 2, cols], p_t[n % 2][:, cols], pt_hi[:, n % 2, cols].bitcast(F32), ALU.subtract).then_inc(lo_done, 1)
                    else:
                        r = rounds[n]
                        k, u0 = r["n"], r["units"][0]
                        wait(dve, exp_done, m, units[r["units"][-1]]["halves"][-1])
                        dve.tensor_reduce(rs[:, u0:u0 + k], sums[:, u0:u0 + k, :], AX.X, ALU.add).then_inc(sum_ready, 1)
                        wait(dve, sum_ready, m, n)
                        dve.reciprocal(rinv[:, u0:u0 + k], rs[:, u0:u0 + k]).then_inc(rinv_ready, 1)
                        wait(dve, or_T, m, n)
                        wait(dve, rinv_ready, m, n)
                        dve.tensor_reduce(osum[:, 0:k, :], p_r[:, 0:k * P].rearrange("p (j x d) -> p j d x", x=2, d=HD), AX.X, ALU.add).then_inc(osum_ready, 1)
                        wait(dve, osum_ready, m, n)
                        if n in (0, NCH // 2):
                            dve.wait_ge(stored[r["s"]], m * 16 + 16)
                        dve.tensor_tensor(orow[:, r["s"], r["tile0"]:r["tile0"] + k, :], osum[:, 0:k, :],
                                          rinv[:, u0:u0 + k].unsqueeze(2).to_broadcast([P, k, HD]), ALU.mult).then_inc(o_ready, 1)


def mod_row(c, group, m):
    return c.mod_dram[group * 64 + m:group * 64 + m + 8, :].rearrange("(o j) p -> o (j p)", o=1).broadcast_to([P, D])


def output_projection(nc, c, a):
    with ExitStack() as ctx:
        sb = lambda n, s, d=F32: ctx.enter_context(nc.sbuf_tensor("d_" + n, s, d))
        sem = stage_semaphores(nc, ctx, "d_")
        w_hi, w_lo = sb("w_hi", [P, KD, D], F32R), sb("w_lo", [P, KD, D], F32R)
        wr = sb("wr", [P, KD, R])
        mix, mixn, junk = sb("mix", [P, D]), sb("mixn", [P, D]), sb("junk", [P, D])
        st = sb("st", [P, 12])
        m32 = sb("m32", [P, KD, P])
        m_hi, m_lo = sb("m_hi", [P, KD, P], F32R), sb("m_lo", [P, KD, P], F32R)
        rows = sb("rows", [P, 2, 3, D])
        x, x2, h2 = sb("x", [P, 2, D]), sb("x2", [P, D]), sb("h2", [P, D])
        hT, lgT = sb("hT", [P, KD, P]), sb("lgT", [R, P])
        p_m = ctx.enter_context(nc.psum_tensor("d_pm", [P, 1024], F32))
        p_o = ctx.enter_context(nc.psum_tensor("d_po", [P, 1024], F32))
        p_t = ctx.enter_context(nc.psum_tensor("d_pt", [P, 1024], F32))
        p_l = ctx.enter_context(nc.psum_tensor("d_pl", [P, 512], F32))
        p_lt = ctx.enter_context(nc.psum_tensor("d_plt", [P, 512], F32))
        (mix_loaded, small_loaded, ssq, ms, ln, rs, mixn_ready, mT_done, m32_act, m32_dve, hi_ready, lo_ready, prod_done,
         gated, x2_ready, x2_stored, ssq2, ms2, ln2, rs2, h2_scaled, h2_ready, h2_stored, hT_done, hT_act, hT_dve, lg_done, lg_out,
         lgT_done, lg_ready, x_zeroed, lg_turning) = map(sem, (
            "mix_loaded", "small_loaded", "ssq", "ms", "ln", "rs", "mixn_ready", "mT_done", "m32_act", "m32_dve", "hi_ready",
            "lo_ready", "prod_done", "gated", "x2_ready", "x2_stored", "ssq2", "ms2", "ln2", "rs2", "h2_scaled", "h2_ready",
            "h2_stored", "hT_done", "hT_act", "hT_dve", "lg_done", "lg_out", "lgT_done", "lg_ready", "x_zeroed", "lg_turning"))
        x_loaded = [sem("x_loaded0"), sem("x_loaded1")]
        chunks = [[(0, D, a["w_out"][0][k * P:(k + 1) * P, :])] for k in range(KD)]
        block = ctx.enter_context(nc.Block())
        load, round_hi, take_lo, split = load_split_weights(ctx, nc, sem, "wd", chunks, w_hi, w_lo, D)
        LAST = NT - 1

        @block.sync
        def _(sp):
            def load_mix(i):
                sp.dma_start(mix[:], c.mix[bass.ds(i, 1)].rearrange("o p d -> (o p) d")).then_inc(mix_loaded, 16)

            load_mix(0)
            load(sp)
            with nc.allow_non_contiguous_dma(reason="router weights, once"):
                for k in range(KD):
                    sp.dma_start(wr[:, k, 0:NG], a["w_rg"][0][k * P:(k + 1) * P, :]).then_inc(small_loaded, 16)
                    sp.dma_start(wr[:, k, NG:].rearrange("p (g e) -> p g e", g=NG), a["w_re"][0][:, k * P:(k + 1) * P, :].rearrange("g p e -> p g e")).then_inc(small_loaded, 16)
            for g in range(2):
                for r, m in enumerate((M_G1, M_SC2, M_SH2)):
                    sp.dma_start(rows[:, g, r, :], mod_row(c, g, m)).then_inc(small_loaded, 16)

            def step(i, s, nxt=True, first=False):
                if nxt:
                    sp.wait_ge(mixn_ready, i + 1)
                    load_mix(i + 1)
                if not first:
                    sp.wait_ge(x2_ready, i - 1)
                if isinstance(i, int) and i == LAST:
                    sp.wait_ge(x_zeroed, 1)
                    sp.dma_start(x[0:DEC, s], a["x_sample"][0]).then_inc(x_loaded[s], 16)
                else:
                    sp.dma_start(x[:, s], a["x_prompt"][0, bass.ds(i * P, P), :]).then_inc(x_loaded[s], 16)

            def store(i):
                sp.wait_ge(x2_ready, i + 1)
                sp.dma_start(c.x2[bass.ds(i, 1)].rearrange("o p d -> (o p) d"), x2[:]).then_inc(x2_stored, 16)
                sp.wait_ge(h2_ready, i + 1)
                sp.dma_start(c.h2[bass.ds(i * P, P), :], h2[:]).then_inc(h2_stored, 16)

            step(0, 0, first=True)
            step(1, 1, first=True)
            with sp.Fori(1, NT_P // 2) as m:
                for s in range(2):
                    store(m * 2 + s - 2)
                    step(m * 2 + s, s)
            store(NT_P - 2)
            step(LAST, 0, nxt=False)
            store(NT_P - 1)
            store(LAST)
            sp.wait_ge(x2_stored, 16 * NT)
            sp.wait_ge(h2_stored, 16 * NT)

        @block.tensor
        def _(pe):
            def turn(i, first=False):
                pe.wait_ge(mixn_ready, i + 2)
                if not first:
                    pe.wait_ge(m32_act, i + 1)
                    pe.wait_ge(m32_dve, i + 1)
                for k in range(KD):
                    last = pe.transpose(p_m[:, k * P:(k + 1) * P], mixn[:, k * P:(k + 1) * P], c.ident[:])
                last.then_inc(mT_done, 1)

            def product(i, first=False):
                if not first:
                    pe.wait_ge(gated, i)
                for half in range(2):
                    cols = slice(half * 512, (half + 1) * 512)
                    for k in range(KD):
                        if half == 0 and k % 4 == 0:
                            pe.wait_ge(lo_ready, i * 2 + 1 + k // 4)
                        last = product3(pe, p_o[:, cols], m_hi[:, k, :], m_lo[:, k, :], w_hi[:, k, cols], w_lo[:, k, cols], k == 0, k == KD - 1)
                last.then_inc(prod_done, 1)

            def route(i, first=False):
                pe.wait_ge(h2_ready, i)
                if not first:
                    pe.wait_ge(hT_act, i - 1)
                    pe.wait_ge(hT_dve, i - 1)
                for k in range(KD):
                    last = pe.transpose(p_t[:, k * P:(k + 1) * P], h2[:, k * P:(k + 1) * P], c.ident[:])
                last.then_inc(hT_done, 1)
                pe.wait_ge(hT_act, i)
                pe.wait_ge(hT_dve, i)
                if not first:
                    pe.wait_ge(lg_out, i - 1)
                for k in range(KD):
                    last = pe.matmul(p_l[0:R, 0:P], wr[:, k, :], hT[:, k, :], start=(k == 0), stop=(k == KD - 1))
                last.then_inc(lg_done, 1)
                pe.wait_ge(lg_out, i)
                if not first:
                    pe.wait_ge(lg_ready, i - 1)
                pe.sem_inc(lg_turning, 1)
                pe.transpose(p_lt[:, 0:R], lgT[:], c.ident[0:R, 0:R]).then_inc(lgT_done, 1)

            turn(-1, first=True)
            pe.wait_ge(split, KD)
            pe.wait_ge(small_loaded, 16 * (2 * KD + 6))
            product(0, first=True)
            turn(0)
            product(1)
            turn(1)
            route(1, first=True)
            with pe.Fori(2, LAST) as i:
                product(i)
                turn(i)
                route(i)
            product(LAST)
            route(LAST)
            route(NT)

        @block.scalar
        def _(act):
            def scale(i):
                act.wait_ge(mix_loaded, i * 16 + 32)
                for half in range(2):
                    cols = slice(half * DS, (half + 1) * DS)
                    last = act.activation(junk[:, cols], mix[:, cols], ACT.Square, accum_out=st[:, half:half + 1])
                last.then_inc(ssq, 1)
                act.wait_ge(ms, i + 2)
                act.activation(st[:, 4:6], st[:, 2:4], ACT.Ln).then_inc(ln, 1)
                act.wait_ge(ln, i + 2)
                act.activation(st[:, 6:8], st[:, 4:6], ACT.Exp, scale=-0.5).then_inc(rs, 1)

            def weigh(i, first=False):
                act.wait_ge(mT_done, i + 2)
                for k in range(4):
                    last = act.activation(m32[:, k, :], p_m[:, k * P:(k + 1) * P], ACT.Copy, scale=c.vcol[:, V_SSDW + k:V_SSDW + k + 1])
                last.then_inc(m32_act, 1)
                if not first:
                    act.wait_ge(prod_done, i + 1)
                act.wait_ge(m32_act, i + 2)
                act.activation(m_hi[:, 0:4, :], m32[:, 0:4, :], ACT.Copy).then_inc(hi_ready, 1)
                act.wait_ge(m32_dve, i + 2)
                act.activation(m_hi[:, 4:8, :], m32[:, 4:8, :], ACT.Copy).then_inc(hi_ready, 1)

            def norm2(i):
                act.wait_ge(x2_ready, i + 1)
                act.activation(junk[:], x2[:], ACT.Square, accum_out=st[:, 8:9]).then_inc(ssq2, 1)
                act.wait_ge(ms2, i + 1)
                act.activation(st[:, 10:11], st[:, 9:10], ACT.Ln).then_inc(ln2, 1)
                act.wait_ge(ln2, i + 1)
                act.activation(st[:, 11:12], st[:, 10:11], ACT.Exp, scale=-0.5).then_inc(rs2, 1)

            def route(i):
                act.wait_ge(hT_done, i)
                act.activation(hT[:, 0:4, :], p_t[:, 0:512].rearrange("p (k t) -> p k t", t=P), ACT.Copy).then_inc(hT_act, 1)
                act.wait_ge(lg_done, i)
                act.activation(lgT[:], p_l[0:R, 0:P], ACT.Copy).then_inc(lg_out, 1)

            scale(-1)
            weigh(-1, first=True)
            round_hi(act)
            scale(0)
            weigh(0)
            norm2(0)
            scale(1)
            weigh(1)
            norm2(1)
            route(1)
            with act.Fori(2, LAST) as i:
                scale(i)
                weigh(i)
                norm2(i)
                route(i)
            norm2(LAST)
            route(LAST)
            route(NT)

        @block.vector
        def _(dve):
            def normalize(i, first=False):
                dve.wait_ge(ssq, i + 2)
                dve.tensor_scalar(st[:, 2:4], st[:, 0:2], 1.0 / DS, EPS, ALU.mult, ALU.add).then_inc(ms, 1)
                dve.wait_ge(rs, i + 2)
                if not first:
                    dve.wait_ge(mT_done, i + 1)
                for half in range(2):
                    cols = slice(half * DS, (half + 1) * DS)
                    last = dve.tensor_scalar(mixn[:, cols], mix[:, cols], st[:, 6 + half:7 + half], None, ALU.mult)
                last.then_inc(mixn_ready, 1)

            def weigh(i, first=False):
                dve.wait_ge(mT_done, i + 2)
                if not first:
                    dve.wait_ge(hi_ready, i * 2 + 2)
                for k in range(4, KD):
                    last = dve.tensor_scalar(m32[:, k, :], p_m[:, k * P:(k + 1) * P], c.vcol[:, V_SSDW + k:V_SSDW + k + 1], None, ALU.mult)
                last.then_inc(m32_dve, 1)
                for half in range(2):
                    ks = slice(4 * half, 4 * half + 4)
                    dve.wait_ge(hi_ready, i * 2 + 3 + half)
                    dve.tensor_tensor(m_lo[:, ks, :], m32[:, ks, :], m_hi[:, ks, :].bitcast(F32), ALU.subtract).then_inc(lo_ready, 1)

            def residual(i, s, loaded, group=0, first=False):
                dve.wait_ge(prod_done, i + 1)
                if not first:
                    dve.wait_ge(x2_stored, i * 16)
                dve.tensor_tensor(x2[:], p_o[:], rows[:, group, 0, :], ALU.mult).then_inc(gated, 1)
                dve.wait_ge(gated, i + 1)
                dve.wait_ge(x_loaded[s], loaded)
                dve.tensor_tensor(x2[:], x2[:], x[:, s, :], ALU.add).then_inc(x2_ready, 1)
                dve.wait_ge(ssq2, i + 1)
                dve.tensor_scalar(st[:, 9:10], st[:, 8:9], 1.0 / D, EPS, ALU.mult, ALU.add).then_inc(ms2, 1)
                dve.wait_ge(rs2, i + 1)
                if not first:
                    dve.wait_ge(h2_stored, i * 16)
                    dve.wait_ge(hT_done, i)
                dve.scalar_tensor_tensor(out=h2[:], in0=x2[:], scalar=st[:, 11:12], in1=rows[:, group, 1, :], op0=ALU.mult, op1=ALU.mult).then_inc(h2_scaled, 1)
                dve.wait_ge(h2_scaled, i + 1)
                dve.tensor_tensor(h2[:], h2[:], rows[:, group, 2, :], ALU.add).then_inc(h2_ready, 1)

            def route(i):
                dve.wait_ge(hT_done, i)
                dve.tensor_copy(hT[:, 4:8, :], p_t[:, 512:1024].rearrange("p (k t) -> p k t", t=P)).then_inc(hT_dve, 1)

            def logits(i):
                dve.wait_ge(lgT_done, i)
                dve.tensor_tensor(c.logits[:, bass.ds(i * R - R, R)], p_lt[:, 0:R], c.b_router[:], ALU.add).then_inc(lg_ready, 1)

            normalize(-1, first=True)
            weigh(-1, first=True)
            take_lo(dve)
            dve.wait_ge(small_loaded, 16 * (2 * KD + 6))
            normalize(0)
            weigh(0)
            residual(0, 0, 16, first=True)
            normalize(1)
            weigh(1)
            route(1)
            residual(1, 1, 16)
            logits(1)

            def body(i, s, loaded):
                normalize(i)
                weigh(i)
                route(i)
                residual(i, s, loaded)
                logits(i)

            with dve.Fori(1, NT_P // 2 - 1) as m:
                for s in range(2):
                    body(m * 2 + s, s, m * 16 + 16)
            body(NT_P - 2, 0, 16 * (NT_P // 2))
            dve.wait_ge(x2_ready, NT_P - 1)
            dve.memset(x[DEC:P, 0, :], 0.0).then_inc(x_zeroed, 1)
            body(NT_P - 1, 1, 16 * (NT_P // 2))
            route(LAST)
            residual(LAST, 0, 16 * (NT_P // 2 + 1), group=1)
            logits(LAST)
            route(NT)
            logits(NT)


def routing(nc, c, a):
    BIG = 1e30
    with ExitStack() as ctx:
        sb = lambda n, s, d=F32: ctx.enter_context(nc.sbuf_tensor("r_" + n, s, d))
        sem = stage_semaphores(nc, ctx, "r_")
        io4, io16 = sb("io4", [P, NG]), sb("io16", [P, NE])
        tok = sb("tok", [P, NT], I32)
        g4, e4, goh, mk = sb("g4", [P, NT, NG]), sb("e4", [P, NT, NG]), sb("goh", [P, NT, NG]), sb("mk", [P, NT, NG])
        v = sb("v", [P, 12, NT])
        ml, t16, oh1, oh2, oh = (sb(n, [P, NT, NE]) for n in ("ml", "t16", "oh1", "oh2", "oh"))
        base, slot = sb("base", [P, NT + 1, NE]), sb("slot", [P, NT, NE])
        nb, nbi, pend, pst = sb("nb", [P, NE]), sb("nbi", [P, NE], I32), sb("pend", [P, NE]), sb("pst", [P, NE])
        dest = sb("dest", [P, NT, 2])
        zero = sb("zero", [P, NBLK + 1], I32)
        p_rank = ctx.enter_context(nc.psum_tensor("r_rank", [P, 512], F32))
        p_tot = ctx.enter_context(nc.psum_tensor("r_tot", [P, 512], F32))
        (iotas, zero_set, zeroed, step_done, e_ready, e2_ready, oh_ready, counted, dest_ready, scattered) = map(sem, (
            "iotas", "zero_set", "zeroed", "step_done", "e_ready", "e2_ready", "oh_ready", "counted", "dest_ready", "scattered"))
        block = ctx.enter_context(nc.Block())
        col = lambda s: v[:, s, :]
        over = lambda t, n: t.unsqueeze(2).to_broadcast([P, NT, n])
        along = lambda t, n: t.unsqueeze(1).to_broadcast([P, NT, n])

        @block.sync
        def _(sp):
            sp.wait_ge(zero_set, 1)
            sp.dma_start(c.slot_tok.rearrange("(p b) o -> p (b o)", p=P), zero[:]).then_inc(zeroed, 16)
            sp.wait_ge(zeroed, 16)

        @block.gpsimd
        def _(pool):
            nc.gpsimd.iota(io4[:], pattern=[[1, NG]], base=0, channel_multiplier=0, allow_small_or_imprecise_dtypes=True)
            nc.gpsimd.iota(io16[:], pattern=[[1, NE]], base=0, channel_multiplier=0, allow_small_or_imprecise_dtypes=True)
            nc.gpsimd.iota(tok[:], pattern=[[P, NT]], base=0, channel_multiplier=1).then_inc(iotas, 1)
            pool.wait_ge(iotas, 1)
            pool.wait_ge(zeroed, 16)
            pool.wait_ge(dest_ready, 1)
            for t in range(NT):
                n = P if t < NT_P else DEC
                for k in range(2):
                    nc.gpsimd.indirect_dma_start(
                        out=c.slot_tok, out_offset=bass.IndirectOffsetOnAxis(ap=c.dest[0:n, 2 * t + k:2 * t + k + 1], axis=0),
                        in_=tok[0:n, t:t + 1], in_offset=None).then_inc(scattered, 16)
            pool.wait_ge(scattered, 16 * 2 * NT)

        @block.tensor
        def _(pe):
            pe.wait_ge(oh_ready, 1)
            flat = oh[:].rearrange("p t e -> p (t e)")
            pe.matmul(p_rank[:, 0:NT * NE], c.tri_strict[:], flat, start=True, stop=True)
            pe.matmul(p_tot[:, 0:NT * NE], c.ones[:], flat, start=True, stop=True).then_inc(counted, 1)

        @block.scalar
        def _(act):
            act.wait_ge(step_done, 2)
            act.activation(e4[:], g4[:], ACT.Exp).then_inc(e_ready, 1)
            act.wait_ge(e2_ready, 1)
            act.activation(col(6), col(5), ACT.Exp).then_inc(e2_ready, 1)

        @block.vector
        def _(dve):
            n = 0

            def then(ins):
                nonlocal n
                n += 1
                ins.then_inc(step_done, 1)
                dve.wait_ge(step_done, n)

            lg = c.logits[:].rearrange("p (t r) -> p t r", r=R)
            gl, el = lg[:, :, 0:NG], lg[:, :, NG:]
            dve.memset(zero[:], 0).then_inc(zero_set, 1)
            then(dve.tensor_reduce(col(0), gl, AX.X, ALU.max))
            then(dve.tensor_tensor(g4[:], gl, over(col(0), NG), ALU.subtract))
            dve.wait_ge(e_ready, 1)
            then(dve.tensor_reduce(col(1), e4[:], AX.X, ALU.add))
            then(dve.reciprocal(col(2), col(1)))
            dve.wait_ge(iotas, 1)

            def first_max(oh_out, val, mx, tmp, iota, width, low):
                then(dve.tensor_tensor(tmp, val, over(mx, width), ALU.is_equal))
                then(dve.scalar_tensor_tensor(out=tmp, in0=tmp, scalar=-float(width), in1=along(iota[:], width), op0=ALU.mult, op1=ALU.add))
                then(dve.tensor_reduce(low, tmp, AX.X, ALU.min))
                then(dve.tensor_tensor(oh_out, tmp, over(low, width), ALU.is_equal))

            first_max(goh[:], gl, col(0), mk[:], io4, NG, col(3))
            then(dve.tensor_scalar(mk[:], goh[:], BIG, -BIG, ALU.mult, ALU.add))
            for g in range(NG):
                es = slice(4 * g, 4 * g + 4)
                wide = lambda t: t[:, :, g:g + 1].to_broadcast([P, NT, 4])
                then(dve.tensor_tensor(ml[:, :, es], el[:, :, es], wide(goh), ALU.mult))
                then(dve.tensor_tensor(ml[:, :, es], ml[:, :, es], wide(mk), ALU.add))
            then(dve.tensor_reduce(col(3), ml[:], AX.X, ALU.max))
            first_max(oh1[:], ml[:], col(3), t16[:], io16, NE, col(8))
            then(dve.scalar_tensor_tensor(out=ml[:], in0=oh1[:], scalar=-3.0 * BIG, in1=ml[:], op0=ALU.mult, op1=ALU.add))
            then(dve.tensor_reduce(col(4), ml[:], AX.X, ALU.max))
            first_max(oh2[:], ml[:], col(4), t16[:], io16, NE, col(8))
            then(dve.tensor_tensor(col(5), col(4), col(3), ALU.subtract))
            dve.sem_inc(e2_ready, 1)
            dve.wait_ge(e2_ready, 2)
            then(dve.tensor_scalar(col(7), col(6), 1.0, None, ALU.add))
            then(dve.reciprocal(col(9), col(7)))
            wt = c.weight[:].rearrange("p (t k) -> p t k", k=2)
            then(dve.tensor_tensor(wt[:, :, 0], col(9), col(2), ALU.mult))
            then(dve.tensor_tensor(wt[:, :, 1], wt[:, :, 0], col(6), ALU.mult))
            then(dve.memset(oh1[DEC:P, NT - 1, :], 0.0))
            then(dve.memset(oh2[DEC:P, NT - 1, :], 0.0))
            dve.tensor_tensor(oh[:], oh1[:], oh2[:], ALU.add).then_inc(oh_ready, 1)
            then(dve.memset(base[:, 0, :], 0.0))
            dve.wait_ge(counted, 1)
            tot = p_tot[:, 0:NT * NE].rearrange("p (t e) -> p t e", e=NE)
            rank = p_rank[:, 0:NT * NE].rearrange("p (t e) -> p t e", e=NE)
            for t in range(NT):
                then(dve.tensor_tensor(base[:, t + 1, :], base[:, t, :], tot[:, t, :], ALU.add))
            then(dve.tensor_scalar(nb[:], base[:, NT, :], float(P - 1), None, ALU.add))
            then(dve.tensor_copy(nbi[:], nb[:]))
            then(dve.tensor_scalar(nbi[:], nbi[:], 7, None, ALU.arith_shift_right))
            then(dve.tensor_copy(nb[:], nbi[:]))
            then(dve.tensor_scalar(nb[:], nb[:], 1.0, None, ALU.max))
            then(dve.tensor_tensor_scan(pend[:], c.ones[:, 0:NE], nb[:], 0.0, ALU.mult, ALU.add))
            then(dve.tensor_tensor(pst[:], pend[:], nb[:], ALU.subtract))
            then(dve.tensor_copy(c.table[:, 0:NE], pst[0:1, :]))
            then(dve.tensor_scalar(nb[:], pend[:], -1.0, None, ALU.add))
            then(dve.tensor_copy(c.table[:, NE:2 * NE], nb[0:1, :]))
            then(dve.tensor_scalar(nb[:], pend[:], 1.0, None, ALU.add))
            then(dve.tensor_copy(c.table[:, 2 * NE:2 * NE + 1], nb[0:1, NE - 1:NE]))
            then(dve.tensor_scalar(nb[:], pend[:], -1.0, float(NBLK + 1), ALU.mult, ALU.add))
            then(dve.tensor_copy(c.table[:, 2 * NE + 1:2 * NE + 2], nb[0:1, NE - 1:NE]))
            then(dve.tensor_scalar(pst[:], pst[:], float(P), None, ALU.mult))
            then(dve.tensor_tensor(slot[:], rank, base[:, 0:NT, :], ALU.add))
            then(dve.tensor_tensor(slot[:], slot[:], along(pst[:], NE), ALU.add))
            for k, o in enumerate((oh1, oh2)):
                then(dve.tensor_tensor(t16[:], o[:], slot[:], ALU.mult))
                then(dve.tensor_reduce(dest[:, :, k], t16[:], AX.X, ALU.add))
            dve.tensor_copy(c.dest[:].rearrange("p (t k) -> p t k", k=2), dest[:]).then_inc(dest_ready, 1)


def experts(nc, c, a):
    KF = FE // P
    with ExitStack() as ctx:
        sb = lambda n, s, d=F32: ctx.enter_context(nc.sbuf_tensor("x_" + n, s, d))
        sem = stage_semaphores(nc, ctx, "e_")
        raw_g, raw_u, raw_d = sb("raw_g", [P, KD, FE]), sb("raw_u", [P, KD, FE]), sb("raw_d", [P, KF, D])
        g_hi, u_hi, d_hi = sb("g_hi", [P, KD, FE], F32R), sb("u_hi", [P, KD, FE], F32R), sb("d_hi", [P, KF, D], F32R)
        g_lo, u_lo, d_lo = sb("g_lo", [P, KD, FE], F32R), sb("u_lo", [P, KD, FE], F32R), sb("d_lo", [P, KF, D], F32R)
        tok, rows = sb("tok", [P, 1], I32), sb("rows", [P, D])
        x_hi, x_lo = sb("x_hi", [P, KD, P], F32R), sb("x_lo", [P, KD, P], F32R)
        sg, hm = sb("sg", [P, FE]), sb("hm", [P, FE])
        m_hi, m_lo = sb("m_hi", [P, KF, P], F32R), sb("m_lo", [P, KF, P], F32R)
        out = sb("out", [P, D])
        ps = lambda n, w: ctx.enter_context(nc.psum_tensor("x_" + n, [P, w], F32))
        p_g, p_u, p_x, p_m, p_d = ps("pg", FE), ps("pu", FE), ps("px", D), ps("pm", FE), ps("pd", D)
        p_xv, p_mv = p_x[:].rearrange("p (k t) -> p k t", t=P), p_m[:].rearrange("p (k t) -> p k t", t=P)
        (tok_loaded, gathered, x_turned, x_rounded, x_split, g_done, u_done, silu_done, hm_ready, hm_turned, hm_rounded,
         hm_split, d_done, out_act, out_dve, stored, g_rounded, u_rounded, d_rounded, g_split, u_split, d_split, gather_go, zeroed) = map(sem, (
            "tok_loaded", "gathered", "x_turned", "x_rounded", "x_split", "g_done", "u_done", "silu_done", "hm_ready",
            "hm_turned", "hm_rounded", "hm_split", "d_done", "out_act", "out_dve", "stored", "g_rounded", "u_rounded",
            "d_rounded", "g_split", "u_split", "d_split", "gather_go", "zeroed"))
        g_loaded, u_loaded, d_loaded = ([sem(f"{w}_loaded{q}") for q in range(2)] for w in "gud")
        block = ctx.enter_context(nc.Block())

        def for_experts(eng, one):
            with eng.Fori(0, NE - 1) as e:
                one(e, True)
            one(NE - 1, False)

        def first_block(eng, e):
            return eng.value_load(c.table[0:1, bass.ds(e, 1)], min_val=0, max_val=NBLK - 1)

        def last_block(eng, e):
            return eng.value_load(c.table[0:1, bass.ds(e + NE, 1)], min_val=0, max_val=NBLK - 1)

        @block.sync
        def _(sp):
            def load(e, first=False):
                for raw, src, n, loaded, split in ((raw_g, a["w_gate"][0], KD, g_loaded, g_split),
                                                   (raw_u, a["w_up"][0], KD, u_loaded, u_split),
                                                   (raw_d, a["w_down"][0], KF, d_loaded, d_split)):
                    w = src[bass.ds(e, 1)].rearrange("o (k p) f -> p (o k) f", p=P)
                    for q in range(2):
                        ks = slice(q * n // 2, (q + 1) * n // 2)
                        if not first:
                            sp.wait_ge(split, e * 2 - 1 + q)
                        sp.dma_start(raw[:, ks, :], w[:, ks, :]).then_inc(loaded[q], 16)

            load(0, first=True)
            with sp.Fori(1, NE) as e:
                load(e)
            unused = sp.value_load(c.table[0:1, 2 * NE + 1:2 * NE + 2], min_val=1, max_val=NBLK)
            with sp.If(unused > 1), sp.Fori(1, unused) as n:
                sp.dma_start(c.y_rows[bass.ds(n * -P + NBLK * P, P), :].rearrange("p (k q) -> p k q", q=P),
                             c.zeros[:].unsqueeze(1).to_broadcast([P, KD, P])).then_inc(zeroed, 16)
                sp.wait_ge(zeroed, n * 16)
                sp.sem_inc(gather_go, 1)

        @block.gpsimd
        def _(pool):
            def gather(n, first=False):
                if not first:
                    pool.wait_ge(gathered, n * 16)
                    pool.sem_inc(gather_go, 1)
                pool.dma_start(tok[:], c.slot_tok[bass.ds(n * P, P), :]).then_inc(tok_loaded, 16)
                pool.wait_ge(tok_loaded, n * 16 + 16)
                if not first:
                    pool.wait_ge(x_turned, n * 2)
                    pool.sem_inc(gather_go, 1)
                nc.gpsimd.indirect_dma_start(out=rows[:], out_offset=None, in_=c.h2,
                                             in_offset=bass.IndirectOffsetOnAxis(ap=tok[:, 0:1], axis=0)).then_inc(gathered, 16)

            total = pool.value_load(c.table[0:1, 2 * NE:2 * NE + 1], min_val=NE, max_val=NBLK + 1)
            gather(0, first=True)
            with pool.Fori(1, total) as n:
                gather(n)

        @block.tensor
        def _(pe):
            def turn(n, half, first=False):
                if half == 0:
                    pe.wait_ge(gathered, n * 16 + 16)
                if not first:
                    pe.wait_ge(x_split, n * 2 - 1 + half)
                for k in range(4 * half, 4 * half + 4):
                    last = pe.transpose(p_x[:, k * P:(k + 1) * P], rows[:, k * P:(k + 1) * P], c.ident[:])
                last.then_inc(x_turned, 1)

            def one_block(n, e):
                for hi, lo, out_, split, done, free in ((g_hi, g_lo, p_g, g_split, g_done, silu_done),
                                                        (u_hi, u_lo, p_u, u_split, u_done, hm_ready)):
                    pe.wait_ge(split, e * 2 + 2)
                    pe.wait_ge(free, n + 1)
                    for k in range(KD):
                        if k % 4 == 0:
                            pe.wait_ge(x_split, n * 2 + 1 + k // 4)
                        last = product3(pe, out_[:], x_hi[:, k, :], x_lo[:, k, :], hi[:, k, :], lo[:, k, :], k == 0, k == KD - 1)
                    last.then_inc(done, 1)
                turn(n + 1, 0)
                pe.wait_ge(hm_ready, n + 2)
                pe.wait_ge(hm_split, n + 1)
                for k in range(KF):
                    last = pe.transpose(p_m[:, k * P:(k + 1) * P], hm[:, k * P:(k + 1) * P], c.ident[:])
                last.then_inc(hm_turned, 1)
                turn(n + 1, 1)
                pe.wait_ge(hm_split, n + 2)
                pe.wait_ge(d_split, e * 2 + 2)
                for half, free in ((0, out_act), (1, out_dve)):
                    cols = slice(half * 512, half * 512 + 512)
                    pe.wait_ge(free, n + 1)
                    for k in range(KF):
                        last = product3(pe, p_d[:, cols], m_hi[:, k, :], m_lo[:, k, :], d_hi[:, k, cols], d_lo[:, k, cols], k == 0, k == KF - 1)
                    last.then_inc(d_done, 1)

            def expert(e, more):
                b0, b1 = first_block(pe, e), last_block(pe, e)
                with pe.If(b0 < b1), pe.Fori(b0, b1) as n:
                    one_block(n, e)
                one_block(b1, e)

            pe.sem_inc(hm_turned, 1)
            turn(0, 0, first=True)
            turn(0, 1, first=True)
            for_experts(pe, expert)

        @block.scalar
        def _(act):
            act.sem_inc(silu_done, 1)
            act.sem_inc(out_act, 1)

            def round_x(n, half):
                act.wait_ge(x_turned, n * 2 + 1 + half)
                ks = slice(4 * half, 4 * half + 4)
                act.activation(x_hi[:, ks, :], p_xv[:, ks, :], ACT.Copy).then_inc(x_rounded, 1)

            def round_w(raw, hi, loaded, rounded, n, e):
                for q in range(2):
                    act.wait_ge(loaded[q], e * 16 + 16)
                    ks = slice(q * n // 2, (q + 1) * n // 2)
                    act.activation(hi[:, ks, :], raw[:, ks, :], ACT.Copy).then_inc(rounded, 1)

            def one_block(n, e, more=False):
                act.wait_ge(g_done, n + 1)
                act.wait_ge(hm_ready, n + 1)
                act.activation(sg[:], p_g[:], ACT.Silu).then_inc(silu_done, 1)
                if more:
                    round_w(raw_g, g_hi, g_loaded, g_rounded, KD, e + 1)
                round_x(n + 1, 0)
                act.wait_ge(hm_turned, n + 2)
                act.activation(m_hi[:], p_mv, ACT.Copy).then_inc(hm_rounded, 1)
                round_x(n + 1, 1)
                if more:
                    round_w(raw_u, u_hi, u_loaded, u_rounded, KD, e + 1)
                act.wait_ge(d_done, n * 2 + 1)
                act.wait_ge(stored, n * 16 + 16)
                act.activation(out[:, 0:512], p_d[:, 0:512], ACT.Copy).then_inc(out_act, 1)
                act.wait_ge(out_act, n + 2)
                act.wait_ge(out_dve, n + 2)
                act.dma_start(c.y_rows[bass.ds(n * P, P), :], out[:]).then_inc(stored, 16)

            def expert(e, more):
                b0, b1 = first_block(act, e), last_block(act, e)
                round_w(raw_d, d_hi, d_loaded, d_rounded, KF, e)
                with act.If(b0 < b1), act.Fori(b0, b1) as n:
                    one_block(n, e)
                one_block(b1, e, more)

            act.sem_inc(stored, 16)
            round_w(raw_g, g_hi, g_loaded, g_rounded, KD, 0)
            round_w(raw_u, u_hi, u_loaded, u_rounded, KD, 0)
            round_x(0, 0)
            round_x(0, 1)
            for_experts(act, expert)
            total = act.value_load(c.table[0:1, 2 * NE:2 * NE + 1], min_val=NE, max_val=NBLK + 1)
            act.wait_ge(stored, total * 16)
            act.sem_inc(silu_done, 1)

        @block.vector
        def _(dve):
            dve.sem_inc(hm_ready, 1)
            dve.sem_inc(hm_split, 1)
            dve.sem_inc(out_dve, 1)

            def split_x(n, half):
                dve.wait_ge(x_rounded, n * 2 + 1 + half)
                ks = slice(4 * half, 4 * half + 4)
                dve.tensor_tensor(x_lo[:, ks, :], p_xv[:, ks, :], x_hi[:, ks, :].bitcast(F32), ALU.subtract).then_inc(x_split, 1)

            def split_w(raw, hi, lo, rounded, split, n, e):
                for q in range(2):
                    dve.wait_ge(rounded, e * 2 + 1 + q)
                    ks = slice(q * n // 2, (q + 1) * n // 2)
                    dve.tensor_tensor(lo[:, ks, :], raw[:, ks, :], hi[:, ks, :].bitcast(F32), ALU.subtract).then_inc(split, 1)

            def one_block(n, e, more=False):
                if more:
                    split_w(raw_g, g_hi, g_lo, g_rounded, g_split, KD, e + 1)
                dve.wait_ge(silu_done, n + 2)
                dve.wait_ge(u_done, n + 1)
                dve.wait_ge(hm_turned, n + 1)
                dve.tensor_tensor(hm[:], sg[:], p_u[:], ALU.mult).then_inc(hm_ready, 1)
                split_x(n + 1, 0)
                dve.wait_ge(hm_rounded, n + 1)
                dve.tensor_tensor(m_lo[:], p_mv, m_hi[:].bitcast(F32), ALU.subtract).then_inc(hm_split, 1)
                split_x(n + 1, 1)
                if more:
                    split_w(raw_u, u_hi, u_lo, u_rounded, u_split, KD, e + 1)
                dve.wait_ge(d_done, n * 2 + 2)
                dve.wait_ge(stored, n * 16 + 16)
                dve.tensor_copy(out[:, 512:1024], p_d[:, 512:1024]).then_inc(out_dve, 1)

            def expert(e, more):
                b0, b1 = first_block(dve, e), last_block(dve, e)
                split_w(raw_d, d_hi, d_lo, d_rounded, d_split, KF, e)
                with dve.If(b0 < b1), dve.Fori(b0, b1) as n:
                    one_block(n, e)
                one_block(b1, e, more)

            split_w(raw_g, g_hi, g_lo, g_rounded, g_split, KD, 0)
            split_w(raw_u, u_hi, u_lo, u_rounded, u_split, KD, 0)
            split_x(0, 0)
            split_x(0, 1)
            for_experts(dve, expert)


def final(nc, c, a):
    with ExitStack() as ctx:
        sb = lambda n, s, d=F32: ctx.enter_context(nc.sbuf_tensor("z_" + n, s, d))
        sem = stage_semaphores(nc, ctx, "z_")
        rows = sb("rows", [P, 2, 3, D])
        y1, y2, x2 = sb("y1", [P, 2, D]), sb("y2", [P, 2, D]), sb("x2", [P, 2, D])
        t, x3, junk, out = sb("t", [P, D]), sb("x3", [P, D]), sb("junk", [P, D]), sb("out", [P, D])
        st = sb("st", [P, 4])
        (rows_loaded, y1_weighed, y_weighed, y_gated, x3_ready, ssq, ms, root, rs, scaled, out_ready, stored, weigh_go) = map(sem, (
            "rows_loaded", "y1_weighed", "y_weighed", "y_gated", "x3_ready", "ssq", "ms", "root", "rs", "scaled",
            "out_ready", "stored", "weigh_go"))
        y_loaded, x2_loaded = ([sem(f"{w}_loaded{s}") for s in range(2)] for w in ("y", "x2"))
        block = ctx.enter_context(nc.Block())
        LAST = NT - 1

        def for_tiles(eng, one):
            with eng.Fori(0, NT_P // 2) as m:
                for s in range(2):
                    one(m * 2 + s, s, m + 1, 0)
            one(LAST, 0, NT_P // 2 + 1, 1)

        @block.sync
        def _(sp):
            for g in range(2):
                for r, m in enumerate((M_G2, M_SCF, M_SHF)):
                    sp.dma_start(rows[:, g, r, :], mod_row(c, g, m)).then_inc(rows_loaded, 16)

            def load(i, s, count, group):
                sp.wait_ge(x3_ready, i + 1)
                sp.dma_start(x2[:, s, :], c.x2[bass.ds(i, 1)].rearrange("o p d -> (o p) d")).then_inc(x2_loaded[s], 16)

            for_tiles(sp, load)

        @block.gpsimd
        def _(pool):
            pool.sem_inc(x3_ready, 2)

            def gather(i):
                if i >= 2:
                    pool.wait_ge(y_weighed, i - 1)
                for k, y in enumerate((y1, y2)):
                    nc.gpsimd.indirect_dma_start(out=y[:, i % 2, :], out_offset=None, in_=c.y_rows,
                                                 in_offset=bass.IndirectOffsetOnAxis(ap=c.dest[:, 2 * i + k:2 * i + k + 1], axis=0)).then_inc(y_loaded[i % 2], 16)

            gather(0)
            for i in range(NT):
                if i + 1 < NT:
                    gather(i + 1)
                pool.wait_ge(y_gated, i + 1)
                pool.wait_ge(x2_loaded[i % 2], 16 * (i // 2 + 1))
                if i >= 1:
                    pool.wait_ge(scaled, i)
                pool.tensor_tensor(x3[:], t[:], x2[:, i % 2, :], ALU.add).then_inc(x3_ready, 1)

        @block.scalar
        def _(act):
            act.sem_inc(stored, 16)

            def one(i, s, count, group):
                act.wait_ge(x3_ready, i + 3)
                act.activation(junk[:], x3[:], ACT.Square, accum_out=st[:, 0:1]).then_inc(ssq, 1)
                act.wait_ge(ms, i + 1)
                act.activation(st[:, 2:3], st[:, 1:2], ACT.Sqrt).then_inc(root, 1)
                act.wait_ge(out_ready, i + 1)
                if group:
                    act.dma_start(a["y_sample"][0], out[0:DEC, :]).then_inc(stored, 16)
                else:
                    act.dma_start(a["y_prompt"][0, bass.ds(i * P, P), :], out[:]).then_inc(stored, 16)

            for_tiles(act, one)
            act.wait_ge(stored, 16 * (NT + 1))

        @block.vector
        def _(dve):
            dve.wait_ge(rows_loaded, 16 * 6)

            def one(i, s, count, group):
                w = lambda k: c.weight[:, bass.ds(i * 2 + k, 1)]
                dve.wait_ge(y_loaded[s], count * 32)
                dve.tensor_scalar(y1[:, s, :], y1[:, s, :], w(0), None, ALU.mult).then_inc(y1_weighed, 1)
                dve.wait_ge(y1_weighed, i + 1)
                dve.wait_ge(x3_ready, i + 2)
                dve.scalar_tensor_tensor(out=t[:], in0=y2[:, s, :], scalar=w(1), in1=y1[:, s, :], op0=ALU.mult, op1=ALU.add).then_inc(y_weighed, 1)
                dve.wait_ge(y_weighed, i + 1)
                dve.tensor_tensor(t[:], t[:], rows[:, group, 0, :], ALU.mult).then_inc(y_gated, 1)
                dve.wait_ge(ssq, i + 1)
                dve.tensor_scalar(st[:, 1:2], st[:, 0:1], 1.0 / D, EPS, ALU.mult, ALU.add).then_inc(ms, 1)
                dve.wait_ge(root, i + 1)
                dve.reciprocal(st[:, 3:4], st[:, 2:3]).then_inc(rs, 1)
                dve.wait_ge(rs, i + 1)
                dve.wait_ge(stored, i * 16 + 16)
                dve.scalar_tensor_tensor(out=out[:], in0=x3[:], scalar=st[:, 3:4], in1=rows[:, group, 1, :], op0=ALU.mult, op1=ALU.mult).then_inc(scaled, 1)
                dve.wait_ge(scaled, i + 1)
                dve.tensor_tensor(out[:], out[:], rows[:, group, 2, :], ALU.add).then_inc(out_ready, 1)

            for_tiles(dve, one)


class Shared:
    pass


def build(nc, a, upto=99):
    c = Shared()
    with ExitStack() as ctx:
        sb = lambda n, s, d=F32: ctx.enter_context(nc.sbuf_tensor(n, s, d))
        dram = lambda n, s, d=F32: nc.dram_tensor(n, s, d).ap()
        c.ident, c.ones, c.zeros = sb("ident", [P, P]), sb("ones", [P, P]), sb("zeros", [P, P])
        c.tri, c.tri_strict = sb("tri", [P, P]), sb("tri_strict", [P, P])
        c.neg_ts, c.neg_qk = sb("neg_ts", [P, P]), sb("neg_qk", [P, P])
        c.sign = sb("sign", [P, 2 * H])
        c.params = sb("params", [P, 4 * H])
        c.neg_a = sb("neg_a", [P, H])
        c.b_router = sb("b_router", [P, R])
        c.vcol = sb("vcol", [P, V_ALL])
        c.mod_t = sb("mod_t", [P, 2, 64])
        c.const_filled = ctx.enter_context(nc.semaphore("const_filled"))
        c.mod_dram = dram("mod_dram", [P, P])
        c.h_hi = dram("h_hi", [NT, P, D])
        c.h_lo = dram("h_lo", [NT, P, D])
        c.mix = dram("mix", [NT, P, D])
        c.f_q, c.f_k = dram("f_q", [H, 4, TP]), dram("f_k", [H, 4, TK])
        c.q_hi, c.q_lo = dram("q_hi", [DS, TP]), dram("q_lo", [DS, TP])
        c.k_hi, c.k_lo = dram("k_hi", [DS, TK]), dram("k_lo", [DS, TK])
        c.v_hl = dram("v_hl", [H, NT_K, P, 2 * HD])
        constants(nc, c)
        modulation(nc, c, a)
        if upto >= 1:
            with ExitStack() as keep:
                c.logf_t = keep.enter_context(nc.sbuf_tensor("logf_t", [H, TP], F32))
                ssd_branch(nc, c, a)
                if upto >= 2:
                    forget_sums(nc, c, a)
            if upto >= 2:
                qkv_projection(nc, c, a)
            if upto >= 3:
                attention(nc, c, a)
            if upto >= 4:
                c.x2, c.h2 = dram("x2", [NT, P, D]), dram("h2", [TP, D])
                c.slot_tok, c.y_rows = dram("slot_tok", [(NBLK + 1) * P, 1], I32), dram("y_rows", [NSLOT, D])
                c.logits = sb("logits", [P, NT * R])
                c.dest, c.weight = sb("dest", [P, NT * 2], U32), sb("weight", [P, NT * 2])
                c.table = sb("table", [1, 2 * NE + 2], I32)
                output_projection(nc, c, a)
                routing(nc, c, a)
            if upto >= 5:
                experts(nc, c, a)
            if upto >= 6:
                final(nc, c, a)


_INS = ['x_prompt', 'x_sample', 'c_prompt', 'c_sample', 'cache_k', 'cache_v', 'cache_logf', 'state_conv', 'state_ssm',
        'norm1_w', 'w_ada', 'b_ada', 'w_in', 'conv_w', 'conv_b', 'dt_bias', 'a_log', 'd_skip', 'ssd_norm_w', 'f_bias',
        'attn_norm_w', 'w_out', 'norm2_w', 'w_rg', 'b_rg', 'w_re', 'b_re', 'w_gate', 'w_up', 'w_down',
        'final_norm_w', 'w_ada_f', 'b_ada_f']
_OUTS = [("y_prompt", (1, SEQ, D)), ("y_sample", (1, DEC, D)),
         ("k_prompt", (1, 1, SEQ, H, HD)), ("v_prompt", (1, 1, SEQ, H, HD)), ("logf_prompt", (1, 1, SEQ, H)),
         ("conv_prompt", (1, 1, CW - 1, DC)), ("ssm_prompt", (1, 1, H, HD, NST)),
         ("k_sample", (1, 1, DEC, H, HD)), ("v_sample", (1, 1, DEC, H, HD)), ("logf_sample", (1, 1, DEC, H)),
         ("conv_sample", (1, 1, CW - 1, DC)), ("ssm_sample", (1, 1, H, HD, NST))]


def kernel(**inputs):
    import numpy as _np
    import concourse.bacc as _bacc
    from concourse import mybir as _mybir
    from concourse.bass_utils import run_bass_kernel_spmd as _run

    nc = _bacc.Bacc("TRN2", target_bir_lowering=False, num_devices=1)
    arrays, aps = {}, {}
    for name in _INS:
        x = _np.ascontiguousarray(inputs[name])
        arrays[f"in_{name}_dram"] = x
        aps[name] = nc.dram_tensor(f"in_{name}_dram", x.shape, _mybir.dt.from_np(x.dtype), kind="ExternalInput").ap()
    for name, shape in _OUTS:
        aps[name] = nc.dram_tensor(f"out_{name}_dram", shape, _mybir.dt.float32, kind="ExternalOutput").ap()
    build(nc, aps)
    r = _run(nc, [arrays], core_ids=[0])
    return tuple(r.results[0][f"out_{name}_dram"] for name, _ in _OUTS)
```
